# Optimizing a Trainium2 kernel written in Bass

```python
import math
import numpy as np
import jax
import jax.numpy as jnp
from jax import lax

D_MODEL = 1024
BATCH = 1
SEQ = 512
DEPTH = 2
DEC_BATCH = 8
DEC_SEQ = 1
PAST_LEN = 4096
PAGE_SIZE = 128

N_MIXERS = 2
N_SSD_LAYERS = (DEPTH + N_MIXERS - 1) // N_MIXERS
N_CM_LAYERS = DEPTH // N_MIXERS

SSD_EXPAND = 2
D_INNER = SSD_EXPAND * D_MODEL
SSD_HEAD_DIM = 64
SSD_HEADS = D_INNER // SSD_HEAD_DIM
SSD_GROUPS = 8
SSD_HPG = SSD_HEADS // SSD_GROUPS
SSD_STATE = 128
SSD_CONV_K = 4
SSD_CHUNK = 128
SSD_CONV_DIM = D_INNER + 2 * SSD_GROUPS * SSD_STATE
SSD_IN_DIM = D_INNER + SSD_CONV_DIM + SSD_HEADS

CM_CHUNK = 128
CM_WIDTH = 2 * D_MODEL
CM_GROUPS = 8
CM_GROUP_DIM = CM_WIDTH // CM_GROUPS

D_FF = 4 * D_MODEL

RMS_EPS = 1e-5

kernel_name = 'hybrid_ssd_chunkmlp_decoder_step'

def rmsnorm(x, g):
    xf = x.astype(jnp.float32)
    r = lax.rsqrt(jnp.mean(xf * xf, axis=-1, keepdims=True) + RMS_EPS)
    return (xf * r * g.astype(jnp.float32)).astype(x.dtype)

def ssd_scan(x, dt, A, B, C, h0):
    b, l = x.shape[:2]
    q = min(SSD_CHUNK, l)
    lp = -(-l // q) * q
    pad = lp - l
    if pad:
        pw = ((0, 0), (0, pad))
        x = jnp.pad(x, pw + ((0, 0), (0, 0)))
        dt = jnp.pad(dt, pw + ((0, 0),))
        B = jnp.pad(B, pw + ((0, 0), (0, 0)))
        C = jnp.pad(C, pw + ((0, 0), (0, 0)))
    nc = lp // q
    xc = x.reshape(b, nc, q, SSD_GROUPS, SSD_HPG, SSD_HEAD_DIM)
    dtc = dt.astype(jnp.float32).reshape(b, nc, q, SSD_GROUPS, SSD_HPG)
    Bc = B.reshape(b, nc, q, SSD_GROUPS, SSD_STATE)
    Cc = C.reshape(b, nc, q, SSD_GROUPS, SSD_STATE)
    a = dtc * A.astype(jnp.float32).reshape(SSD_GROUPS, SSD_HPG)
    a_cum = jnp.cumsum(a, axis=2)
    xdt = xc * dtc[..., None]
    ac = jnp.moveaxis(a_cum, 2, -1)
    seg = ac[..., :, None] - ac[..., None, :]
    causal = np.tril(np.ones((q, q), dtype=bool))
    decay = jnp.exp(jnp.where(causal, seg, -jnp.inf))
    cb = jnp.einsum('bcqgn,bcsgn->bcgqs', Cc, Bc)
    y_diag = jnp.einsum('bcgrqs,bcsgrp->bcqgrp', cb[:, :, :, None] * decay, xdt)
    decay_to_end = jnp.exp(a_cum[:, :, -1:] - a_cum)
    chunk_states = jnp.einsum('bcsgn,bcsgr,bcsgrp->bcgrpn', Bc, decay_to_end, xdt)
    chunk_decay = jnp.exp(a_cum[:, :, -1])

    def step(h, inp):
        s, d = inp
        return h * d[..., None, None] + s, h

    h_final, h_prev = lax.scan(step, h0.astype(jnp.float32),
                               (jnp.moveaxis(chunk_states, 1, 0), jnp.moveaxis(chunk_decay, 1, 0)))
    h_prev = jnp.moveaxis(h_prev, 0, 1)
    y_off = jnp.einsum('bcqgn,bcgrpn,bcqgr->bcqgrp', Cc, h_prev, jnp.exp(a_cum))
    y = (y_diag + y_off).reshape(b, lp, SSD_HEADS, SSD_HEAD_DIM)[:, :l]
    return y, h_final

def mamba2_mixer(h, conv_buf, ssm_state, w_in, conv_w, conv_b, dt_bias, a_log, d_skip, norm_g, w_out):
    b, l, _ = h.shape
    proj = h @ w_in
    z = proj[..., :D_INNER]
    xbc = proj[..., D_INNER:D_INNER + SSD_CONV_DIM]
    dt_raw = proj[..., D_INNER + SSD_CONV_DIM:]
    xbc_ext = jnp.concatenate([conv_buf.astype(xbc.dtype), xbc], axis=1)
    conv = conv_b + xbc_ext[:, 0:l] * conv_w[0]
    for k in range(1, SSD_CONV_K):
        conv = conv + xbc_ext[:, k:k + l] * conv_w[k]
    new_conv = xbc_ext[:, -(SSD_CONV_K - 1):]
    xbc_act = jax.nn.silu(conv)
    xs = xbc_act[..., :D_INNER].reshape(b, l, SSD_HEADS, SSD_HEAD_DIM)
    gn = SSD_GROUPS * SSD_STATE
    Bm = xbc_act[..., D_INNER:D_INNER + gn].reshape(b, l, SSD_GROUPS, SSD_STATE)
    Cm = xbc_act[..., D_INNER + gn:].reshape(b, l, SSD_GROUPS, SSD_STATE)
    dt = jax.nn.softplus(dt_raw.astype(jnp.float32) + dt_bias.astype(jnp.float32))
    A = -jnp.exp(a_log.astype(jnp.float32))
    h0 = ssm_state.reshape(b, SSD_GROUPS, SSD_HPG, SSD_HEAD_DIM, SSD_STATE)
    y, h_final = ssd_scan(xs, dt, A, Bm, Cm, h0)
    y = y + xs * d_skip[:, None]
    y = y.reshape(b, l, D_INNER) * jax.nn.silu(z)
    yg = y.astype(jnp.float32).reshape(b, l, SSD_GROUPS, D_INNER // SSD_GROUPS)
    yg = yg * lax.rsqrt(jnp.mean(yg * yg, axis=-1, keepdims=True) + RMS_EPS)
    y = (yg.reshape(b, l, D_INNER) * norm_g).astype(h.dtype)
    new_ssm = h_final.reshape(b, SSD_HEADS, SSD_HEAD_DIM, SSD_STATE)
    return y @ w_out, new_conv, new_ssm

def chunk_mlp_mixer(h, chunk_len, pos, w_in, b_in, v_g, w_s, b_s, w_out):
    b, l, _ = h.shape
    n = l // chunk_len
    gz = jax.nn.gelu(h @ w_in + b_in, approximate=False)
    u = gz[..., :CM_WIDTH]
    v = rmsnorm(gz[..., CM_WIDTH:], v_g)
    mask = np.tril(np.ones((chunk_len, chunk_len), dtype=bool))
    w = jnp.where(mask, w_s[:, pos][:, :, pos], 0)
    vc = v.reshape(b, n, chunk_len, CM_GROUPS, CM_GROUP_DIM)
    s = jnp.einsum('gts,bnsgd->bntgd', w, vc) + b_s[:, pos].T[:, :, None]
    out = u * s.reshape(b, l, CM_WIDTH).astype(u.dtype)
    return out @ w_out, v

def squared_relu_mlp(h, w_up, w_down):
    a = jax.nn.relu(h @ w_up)
    return (a * a) @ w_down

def trunk(x, conv0, ssm0, chunk_len, pos, p):
    new_conv, new_ssm, new_v = [], [], []
    for i in range(DEPTH):
        j = i // N_MIXERS
        h = rmsnorm(x, p['norm_mix_g'][i])
        if i % N_MIXERS == 0:
            out, c, s = mamba2_mixer(h, conv0[j], ssm0[j], p['ssd_w_in'][j], p['ssd_conv_w'][j],
                                     p['ssd_conv_b'][j], p['ssd_dt_bias'][j], p['ssd_a_log'][j],
                                     p['ssd_d'][j], p['ssd_norm_g'][j], p['ssd_w_out'][j])
            new_conv.append(c)
            new_ssm.append(s)
        else:
            out, v = chunk_mlp_mixer(h, chunk_len, pos, p['cm_w_in'][j], p['cm_b_in'][j],
                                     p['cm_v_norm_g'][j], p['cm_w_s'][j], p['cm_b_s'][j],
                                     p['cm_w_out'][j])
            new_v.append(v)
        x = x + out.astype(x.dtype)
        h2 = rmsnorm(x, p['norm_mlp_g'][i])
        x = x + squared_relu_mlp(h2, p['mlp_w_up'][i], p['mlp_w_down'][i]).astype(x.dtype)
    y = rmsnorm(x, p['norm_final_g'])
    return y, jnp.stack(new_conv), jnp.stack(new_ssm), jnp.stack(new_v)

def setup_inputs(seed: int = 0) -> dict:
    key = jax.random.key(seed)
    ks = jax.random.split(key, 24)
    f32 = jnp.float32
    nrm = lambda k, shape, scale: jax.random.normal(k, shape, f32) * scale
    x_prompt = nrm(ks[0], (BATCH, SEQ, D_MODEL), 1.0)
    x_sample = nrm(ks[1], (DEC_BATCH, DEC_SEQ, D_MODEL), 1.0)
    state_ssm = nrm(ks[2], (N_SSD_LAYERS, DEC_BATCH, SSD_HEADS, SSD_HEAD_DIM, SSD_STATE), 0.5)
    state_conv = nrm(ks[3], (N_SSD_LAYERS, DEC_BATCH, SSD_CONV_K - 1, SSD_CONV_DIM), 1.0)
    norm_mix_g = 1.0 + nrm(ks[4], (DEPTH, D_MODEL), 0.02)
    norm_mlp_g = 1.0 + nrm(ks[5], (DEPTH, D_MODEL), 0.02)
    norm_final_g = 1.0 + nrm(ks[6], (D_MODEL,), 0.02)
    ssd_w_in = nrm(ks[7], (N_SSD_LAYERS, D_MODEL, SSD_IN_DIM), D_MODEL ** -0.5)
    ssd_conv_w = nrm(ks[8], (N_SSD_LAYERS, SSD_CONV_K, SSD_CONV_DIM), SSD_CONV_K ** -0.5)
    ssd_conv_b = nrm(ks[9], (N_SSD_LAYERS, SSD_CONV_DIM), 0.01)
    u = jax.random.uniform(ks[10], (N_SSD_LAYERS, SSD_HEADS), f32)
    dt0 = jnp.exp(u * (math.log(0.1) - math.log(0.001)) + math.log(0.001))
    ssd_dt_bias = dt0 + jnp.log(-jnp.expm1(-dt0))
    ssd_a_log = jnp.log(jax.random.uniform(ks[11], (N_SSD_LAYERS, SSD_HEADS), f32, 1.0, 16.0))
    ssd_d = 1.0 + nrm(ks[12], (N_SSD_LAYERS, SSD_HEADS), 0.1)
    ssd_norm_g = 1.0 + nrm(ks[13], (N_SSD_LAYERS, D_INNER), 0.02)
    ssd_w_out = nrm(ks[14], (N_SSD_LAYERS, D_INNER, D_MODEL), D_INNER ** -0.5)
    cm_w_in = nrm(ks[15], (N_CM_LAYERS, D_MODEL, 2 * CM_WIDTH), D_MODEL ** -0.5)
    cm_b_in = nrm(ks[16], (N_CM_LAYERS, 2 * CM_WIDTH), 0.01)
    cm_v_norm_g = 1.0 + nrm(ks[17], (N_CM_LAYERS, CM_WIDTH), 0.02)
    row_scale = (jnp.arange(CM_CHUNK, dtype=f32) + 1.0) ** -0.5
    cm_w_s = nrm(ks[18], (N_CM_LAYERS, CM_GROUPS, CM_CHUNK, CM_CHUNK), 1.0) * row_scale[:, None]
    cm_b_s = 1.0 + nrm(ks[19], (N_CM_LAYERS, CM_GROUPS, CM_CHUNK), 0.1)
    cm_w_out = nrm(ks[20], (N_CM_LAYERS, CM_WIDTH, D_MODEL), CM_WIDTH ** -0.5)
    mlp_w_up = nrm(ks[21], (DEPTH, D_MODEL, D_FF), D_MODEL ** -0.5)
    mlp_w_down = nrm(ks[22], (DEPTH, D_FF, D_MODEL), D_FF ** -0.5)
    return {'x_prompt': x_prompt, 'x_sample': x_sample, 'state_ssm': state_ssm,
            'state_conv': state_conv, 'norm_mix_g': norm_mix_g, 'norm_mlp_g': norm_mlp_g,
            'norm_final_g': norm_final_g, 'ssd_w_in': ssd_w_in, 'ssd_conv_w': ssd_conv_w,
            'ssd_conv_b': ssd_conv_b, 'ssd_dt_bias': ssd_dt_bias, 'ssd_a_log': ssd_a_log,
            'ssd_d': ssd_d, 'ssd_norm_g': ssd_norm_g, 'ssd_w_out': ssd_w_out,
            'cm_w_in': cm_w_in, 'cm_b_in': cm_b_in, 'cm_v_norm_g': cm_v_norm_g,
            'cm_w_s': cm_w_s, 'cm_b_s': cm_b_s, 'cm_w_out': cm_w_out,
            'mlp_w_up': mlp_w_up, 'mlp_w_down': mlp_w_down}

def reference(x_prompt, x_sample, state_ssm, state_conv, norm_mix_g, norm_mlp_g, norm_final_g,
              ssd_w_in, ssd_conv_w, ssd_conv_b, ssd_dt_bias, ssd_a_log, ssd_d, ssd_norm_g,
              ssd_w_out, cm_w_in, cm_b_in, cm_v_norm_g, cm_w_s, cm_b_s, cm_w_out,
              mlp_w_up, mlp_w_down):
    p = {'norm_mix_g': norm_mix_g, 'norm_mlp_g': norm_mlp_g, 'norm_final_g': norm_final_g,
         'ssd_w_in': ssd_w_in, 'ssd_conv_w': ssd_conv_w, 'ssd_conv_b': ssd_conv_b,
         'ssd_dt_bias': ssd_dt_bias, 'ssd_a_log': ssd_a_log, 'ssd_d': ssd_d,
         'ssd_norm_g': ssd_norm_g, 'ssd_w_out': ssd_w_out, 'cm_w_in': cm_w_in,
         'cm_b_in': cm_b_in, 'cm_v_norm_g': cm_v_norm_g, 'cm_w_s': cm_w_s, 'cm_b_s': cm_b_s,
         'cm_w_out': cm_w_out, 'mlp_w_up': mlp_w_up, 'mlp_w_down': mlp_w_down}
    b = x_prompt.shape[0]
    conv0 = jnp.zeros((N_SSD_LAYERS, b, SSD_CONV_K - 1, SSD_CONV_DIM), x_prompt.dtype)
    ssm0 = jnp.zeros((N_SSD_LAYERS, b, SSD_HEADS, SSD_HEAD_DIM, SSD_STATE), jnp.float32)
    y_prompt, conv_p, ssm_p, _ = trunk(x_prompt, conv0, ssm0, CM_CHUNK, np.arange(CM_CHUNK), p)
    pos_s = (PAST_LEN + np.arange(DEC_SEQ)) % CM_CHUNK
    y_sample, conv_s, ssm_s, v_s = trunk(x_sample, state_conv, state_ssm, DEC_SEQ, pos_s, p)
    return (y_prompt, y_sample, ssm_p, conv_p, ssm_s, conv_s, v_s)


_drawn_inputs = setup_inputs


def setup_inputs(seed=0):
    import zlib

    import numpy as np

    out = dict(_drawn_inputs(seed))
    spreads = {}
    factors = {'norm_final_g': 20.356,
     'ssd_conv_b': 3.317,
     'ssd_norm_g': 3.234,
     'cm_b_in': 5.548,
     'cm_v_norm_g': 22.496,
     'norm_mlp_g': 4.882,
     'cm_b_s': 22.548}
    for name, (base, spread) in spreads.items():
        noise = np.random.default_rng([zlib.crc32(name.encode()), seed]).standard_normal(out[name].shape)
        drawn = base * np.exp(spread * noise) if base else spread * noise
        out[name] = jnp.asarray(drawn.astype(out[name].dtype))
    for name, factor in factors.items():
        out[name] = (out[name] * factor).astype(out[name].dtype)
    return out
```

```python
from contextlib import ExitStack

import concourse.bass as bass
from concourse import mybir

F32 = mybir.dt.float32
F32R = mybir.dt.float32r
ACT = mybir.ActivationFunctionType
ALU = mybir.AluOpType
AX = mybir.AxisListType

P = 128
D = 1024
KT = D // P
TP = 512
NS = 8
T = TP + NS
TH = T // 2
CH = 128
NC = TP // CH
DI = 2048
HEADS = 32
GROUPS = 8
HD = 64
N = 128
CONVD = DI + 2 * GROUPS * N
TAPS = 4
CMW = 2048
FF = 4096
EPS = 1e-5
RAW = TAPS - 1 + TP + NS * TAPS
CONV_N = RAW - TAPS + 1
S0 = TP + TAPS - 1
CHUNKS = FF // D

EVEN = ((0, TH), (TH, TH))
PROMPT = ((0, 256), (256, T - 256))


class Pair:

    def __init__(self, s, loop=0):
        self.s, self.loop = s, loop
        self.slot = s % 2

    def times(self, k, c):
        return self.loop * (2 * k) + (k * self.s + c)

    def unit(self, half, c=0):
        return self.times(2, c) if half else self.times(2, c - 1)

    def use(self, c=0):
        return self.loop + (self.s // 2 + c)

    def next(self, k=1):
        return Pair(self.s + k, self.loop)


J_DT = 0
J_OUT0 = 1 + 3 * 6
J_OUT1 = J_OUT0 + 4 + 3 * 2
J_MLP0 = J_OUT1 + 4
J_V = J_MLP0 + 8 * CHUNKS
J_U0 = J_V + 8
J_CMO0 = J_U0 + 4
J_U1 = J_CMO0 + 4
J_CMO1 = J_U1 + 4
J_MLP1 = J_CMO1 + 4
J_END = J_MLP1 + 8 * CHUNKS


def group_pair(g):
    return 1 + 3 * g + (4 if g >= 6 else 0)


def c_columns(pair):
    groups = {group_pair(g): g for g in range(GROUPS)}
    return 16 * (groups[pair.s] + 1) if pair.s in groups and isinstance(pair.loop, int) else 0


def hybrid_step(nc, x_prompt, x_sample, state_ssm, state_conv, norm_mix_g, norm_mlp_g,
                norm_final_g, ssd_w_in, ssd_conv_w, ssd_conv_b, ssd_dt_bias, ssd_a_log, ssd_d,
                ssd_norm_g, ssd_w_out, cm_w_in, cm_b_in, cm_v_norm_g, cm_w_s, cm_b_s, cm_w_out,
                mlp_w_up, mlp_w_down, y_prompt, y_sample, ssm_prompt, conv_prompt, ssm_sample,
                conv_sample, cm_v_sample):
    ctx = ExitStack()
    with ctx:
        def sb(name, shape, dt=F32):
            return ctx.enter_context(nc.sbuf_tensor(name, shape, dt))

        def sem(name):
            return ctx.enter_context(nc.semaphore(name))

        xT = sb("xT", [P, KT, T])
        h_hi = sb("h_hi", [P, KT, T], F32R)
        h_lo = sb("h_lo", [P, KT, T], F32R)
        a_hi = sb("a_hi", [P, KT, T], F32R)
        a_lo = sb("a_lo", [P, KT, T], F32R)
        w32 = sb("w32", [P, 2, KT, 256])
        w_hi = sb("w_hi", [P, 2, KT, 256], F32R)
        w_lo = sb("w_lo", [P, 2, KT, 256], F32R)
        rstd = sb("rstd", [P, T])
        ssum = sb("ssum", [P, T])
        sq = sb("sq", [P, 2, T])
        work = sb("work", [P, 2, T])
        ident = sb("ident", [P, P])
        causal = sb("causal", [P, P])
        ones = sb("ones", [P, 1])
        eps = sb("eps", [P, 1])
        FEAT = 40 + 16 + 32 + 16
        feat = sb("feat", [P, FEAT])
        CW = 5 + 3 * NS
        convf = sb("convf", [P, 32, CW])
        tokS = sb("tokS", [P, 3, NC, HEADS])
        dtf = sb("dtf", [P, 16, 20])
        cdec = sb("cdec", [P, HEADS, NC])
        ARENA = 14472
        arena = sb("arena", [P, ARENA])

        G_MIX, G_MLP, G_FIN, G_SSD, B_CM, G_V = 0, 16, 32, 40, 56, 88

        at = [0]

        def carve(*shape, parts=P):
            n = 1
            for d in shape:
                n *= d
            ap = arena[0:parts, at[0]:at[0] + n]
            at[0] += n
            assert at[0] <= ARENA, at[0]
            if len(shape) == 2:
                return ap.rearrange("p (a b) -> p a b", a=shape[0])
            if len(shape) == 3:
                return ap.rearrange("p (a b c) -> p a b c", a=shape[0], b=shape[1])
            return ap

        act = carve(2, 4, CONV_N)
        raw = carve(2, RAW + 1)
        dt_at = at[0]
        zs = carve(2, 2, T)
        abc = carve(2, TP)
        xdt = carve(NC, 4 * HD)
        Btok = carve(NC, N)
        cbm = carve(NC, CH)
        hprev = carve(NC, 4 * HD)
        hst = carve(4, N)
        outer = carve(4, N)
        bcs = carve(4, 2 * N)
        cstage = carve(4, P, parts=35)
        bcrow = arena[64:72, at[0] - 512:at[0] - 256]
        ssm_stage = carve(2, N)
        xdts = carve(2, NS)
        ysmp = carve(2, NS)
        at[0] = dt_at
        dt_v = carve(T, parts=HEADS)
        dt_e = carve(T, parts=HEADS)
        dt_dt = carve(T, parts=HEADS)
        dt_a = carve(T, parts=HEADS)
        dt_end = carve(NC, CH, parts=HEADS)
        dt_small = carve(24, parts=HEADS)
        dt_par = carve(4, parts=HEADS)
        dt_one = carve(CH, parts=HEADS)
        at[0] = 0
        xtok = carve(NC, D)
        xs_row = carve(D, parts=NS)
        crow = carve(32, P, parts=CW)
        frow = carve(P, parts=FEAT)
        at[0] = 0
        vtok = carve(NC, CMW)
        wmix = carve(8, CH)
        wmixT = carve(8, CH)
        bmix = carve(8, CH)
        gv = carve(2, T)
        vsmp = carve(16, NS)
        ssmp = carve(16, NS)
        w00 = carve(8, 2)
        r_tok = carve(4)
        r_smp = carve(NS)
        vs_row = carve(4, P, parts=NS)
        at[0] = 0
        ytok = carve(NC, D)
        ys_row = carve(D, parts=NS)
        xg = carve(2, T)
        r_fin = carve(8)

        ps = ctx.enter_context(nc.psum_tensor("ps", [P, 8, 512], F32))

        def psum_tok(slot):
            return ps[:, 2 * slot:2 * slot + 2, 0:TH]

        def halves(ap):
            return ap.rearrange("p (a b) -> p a b", a=2)

        scr_a = nc.dram_tensor("scr_a", (HEADS, TP), F32, kind="Internal").ap()
        scr_s = nc.dram_tensor("scr_s", (HEADS, 24), F32, kind="Internal").ap()
        scr_bc = nc.dram_tensor("scr_bc", (GROUPS, NS, 2 * N), F32, kind="Internal").ap()

        w_landed = [sem("w_landed0"), sem("w_landed1")]
        c_landed = sem("c_landed")
        w_hi_done = sem("w_hi_done")
        w_lo_done = sem("w_lo_done")
        unit_done = sem("unit_done")
        evac_done = sem("evac_done")
        h_hi_ready = sem("h_hi_ready")
        h_lo_ready = sem("h_lo_ready")
        sq_ready = sem("sq_ready")
        ssum_added = sem("ssum_added")
        stats_done = sem("stats_done")
        root_done = sem("root_done")
        r_ready = sem("r_ready")
        x_landed = sem("x_landed")
        xs_landed = sem("xs_landed")
        crow_landed = sem("crow_landed")
        frow_landed = sem("frow_landed")
        par_landed = sem("par_landed")
        ident_ready = sem("ident_ready")
        const_ready = sem("const_ready")
        w_cleared = sem("w_cleared")
        xt_done = sem("xt_done")
        crow_done = sem("crow_done")
        frow_done = sem("frow_done")
        x_ready = sem("x_ready")
        xs_ready = sem("xs_ready")
        convf_ready = sem("convf_ready")
        feat_ready = sem("feat_ready")
        raw_zeroed = sem("raw_zeroed")
        dt_act_done = sem("dt_act_done")
        dt_vec_done = sem("dt_vec_done")
        dt_tr_done = sem("dt_tr_done")
        dt_tok_done = sem("dt_tok_done")
        scr_a_done = sem("scr_a_done")
        scr_s_done = sem("scr_s_done")
        dtf_landed = sem("dtf_landed")
        cdec_landed = sem("cdec_landed")
        sraw_filled = sem("sraw_filled")
        new_evac = sem("new_evac")
        tap0_done = sem("tap0_done")
        tap_done = sem("tap_done")
        silu_done = sem("silu_done")
        z_silu_done = sem("z_silu_done")
        cst_tr = sem("cst_tr")
        cst_evac = sem("cst_evac")
        cst_out = sem("cst_out")
        xtr_done = sem("xtr_done")
        xdt_done = sem("xdt_done")
        Btr_done = sem("Btr_done")
        Btok_done = sem("Btok_done")
        cb_done = sem("cb_done")
        cbm_done = sem("cbm_done")
        bc_tr = sem("bc_tr")
        bc_evac = sem("bc_evac")
        bc_out = sem("bc_out")
        bcs_landed = sem("bcs_landed")
        xdts_done = sem("xdts_done")
        hst_landed = sem("hst_landed")
        outer_done = sem("outer_done")
        decay_done = sem("decay_done")
        snew_done = sem("snew_done")
        sstored = sem("sstored")
        smul_done = sem("smul_done")
        sred_done = sem("sred_done")
        abc_landed = sem("abc_landed")
        seg_done = sem("seg_done")
        exp_done = sem("exp_done")
        m_done = sem("m_done")
        ydiag_done = sem("ydiag_done")
        y1_done = sem("y1_done")
        xdte_done = sem("xdte_done")
        st_done = sem("st_done")
        hstep_done = sem("hstep_done")
        yoff_done = sem("yoff_done")
        ef_landed = sem("ef_landed")
        ef_done = sem("ef_done")
        comb_done = sem("comb_done")
        ysq_done = sem("ysq_done")
        ysum_done = sem("ysum_done")
        rms_done = sem("rms_done")
        yroot_done = sem("yroot_done")
        yr_done = sem("yr_done")
        ynorm_done = sem("ynorm_done")
        y_hi_done = sem("y_hi_done")
        y_lo_done = sem("y_lo_done")
        h4_tr = sem("h4_tr")
        h4_evac = sem("h4_evac")
        ssm_out = sem("ssm_out")
        conv_old = sem("conv_old")
        a_hi_done = sem("a_hi_done")
        a_lo_done = sem("a_lo_done")
        a32_done = sem("a32_done")
        mix_landed = sem("mix_landed")
        mixT_done = sem("mixT_done")
        wmask_done = sem("wmask_done")
        b_landed = sem("b_landed")
        gelu_done = sem("gelu_done")
        v_tr = sem("v_tr")
        vtok_done = sem("vtok_done")
        vsq_done = sem("vsq_done")
        vsum_done = sem("vsum_done")
        vstat_done = sem("vstat_done")
        vroot_done = sem("vroot_done")
        vrec_done = sem("vrec_done")
        vscaled = sem("vscaled")
        vsmp_done = sem("vsmp_done")
        ssmp_done = sem("ssmp_done")
        s_done = sem("s_done")
        mixed = sem("mixed")
        gate_done = sem("gate_done")
        vsn_done = sem("vsn_done")
        y_scaled = sem("y_scaled")
        cchain = sem("cchain")
        hchain = sem("hchain")
        vs_tr = sem("vs_tr")
        vs_evac = sem("vs_evac")
        vs_out = sem("vs_out")
        ty_done = sem("ty_done")
        ty_evac = sem("ty_evac")
        fin_stat = sem("fin_stat")
        fin_root = sem("fin_root")
        fin_rec = sem("fin_rec")
        xg_done = sem("xg_done")
        out_done = sem("out_done")

        def due(count):
            return not isinstance(count, int) or count > 0

        block = ctx.enter_context(nc.Block())

        def w_block(dram, row0, col0, n=256):
            return dram[bass.ds(row0, D), bass.ds(col0, n)].rearrange("(k p) n -> p k n", p=P)

        w_in, w_out = ssd_w_in[0], ssd_w_out[0]
        c_in, c_out = cm_w_in[0], cm_w_out[0]

        @block.sync
        def _(sp):
            def stage(pair, src, dst=None):
                if due(pair.times(1, -1)):
                    sp.wait_ge(w_hi_done, pair.times(1, -1))
                if due(pair.times(1, -1)):
                    sp.wait_ge(w_lo_done, pair.times(1, -1))
                sp.dma_start(w32[:, pair.slot] if dst is None else dst, src).then_inc(w_landed[pair.slot], 16)

            def group(g):
                J = group_pair(g)
                stage(Pair(J), w_block(w_in, 0, 2 * DI + g * N, N), w32[:, J % 2, :, 0:N])
                sp.dma_start(w32[:, J % 2, :, N:2 * N], w_block(w_in, 0, 2 * DI + (GROUPS + g) * N, N))\
                  .then_inc(c_landed, 16)
                stage(Pair(J + 1), w_block(w_in, 0, DI + g * 256))
                stage(Pair(J + 2), w_block(w_in, 0, g * 256))

            def run(J, dram, row0, col0, n):
                for i in range(n):
                    stage(Pair(J + i), w_block(dram, row0, col0 + 256 * i))

            def mlp(J, layer):
                up, down = mlp_w_up[layer], mlp_w_down[layer]
                with sp.Fori(0, CHUNKS) as c:
                    for i in range(4):
                        stage(Pair(J + i, c * 4), w_block(up, 0, c * D + 256 * i))
                    for i in range(4):
                        stage(Pair(J + 4 + i, c * 4), w_block(down, c * D, 256 * i))

            for c in range(NC):
                sp.dma_start(xtok[:, c, :], x_prompt[0, c * P:(c + 1) * P, :]).then_inc(x_landed, 16)
            sp.wait_ge(w_cleared, 1)
            sp.dma_start(w32[:, 0, :, 0:HEADS], w_block(w_in, 0, DI + CONVD, HEADS)).then_inc(w_landed[0], 16)
            for g in range(6):
                group(g)
            run(J_OUT0, w_out, 0, 0, 4)
            group(6)
            group(7)
            run(J_OUT1, w_out, D, 0, 4)
            mlp(J_MLP0, 0)
            run(J_V, c_in, 0, CMW, 8)
            run(J_U0, c_in, 0, 0, 4)
            run(J_CMO0, c_out, 0, 0, 4)
            run(J_U1, c_in, 0, D, 4)
            run(J_CMO1, c_out, D, 0, 4)
            mlp(J_MLP1, 1)
            for c in range(NC):
                sp.wait_ge(y_scaled, c + 1)
                sp.dma_start(y_prompt[0, c * P:(c + 1) * P, :], ytok[:, c, :]).then_inc(out_done, 16)
            sp.wait_ge(y_scaled, NC + 1)
            sp.dma_start(y_sample.rearrange("b s d -> (b s) d"), ys_row[:, :]).then_inc(out_done, 16)
            sp.wait_ge(out_done, 80)

        @block.tensor
        def _(pe):
            def unit(pair, half, hi, lo, split=EVEN, k_ready=None):
                only = pair.s == J_DT and isinstance(pair.loop, int)
                if half == 0 or only:
                    pe.wait_ge(w_hi_done, pair.times(1, 1))
                    pe.wait_ge(w_lo_done, pair.times(1, 1))
                if due(pair.unit(half, -1)):
                    pe.wait_ge(evac_done, pair.unit(half, -1))
                slot, col = 1 - half, 0 if only else half * P
                for k in range(KT):
                    if k_ready:
                        k_ready(k)
                    for n, (w, x) in enumerate(((w_hi, hi), (w_hi, lo), (w_lo, hi))):
                        for b, (t0, tn) in enumerate(split):
                            mm = pe.matmul(ps[:, 2 * slot + b, 0:tn],
                                           w[:, pair.slot, k, col:col + P],
                                           x[:, k, t0:t0 + tn],
                                           start=(k == 0 and n == 0),
                                           stop=(k == KT - 1 and n == 2))
                mm.then_inc(unit_done, 1)

            def h_ready(n):
                def ready(k):
                    pe.wait_ge(h_hi_ready, 8 * n + k + 1)
                    pe.wait_ge(h_lo_ready, 8 * n + k + 1)
                return ready

            def stats(n):
                pe.wait_ge(ssum_added, 7 * (n + 1))
                if due(n):
                    pe.wait_ge(root_done, n)
                if n == 1:
                    pe.wait_ge(comb_done, 16)
                    pe.wait_ge(h4_evac, 8)
                if n == 3:
                    pe.wait_ge(s_done, 16)
                for b in range(2):
                    mm = pe.matmul(ps[:, 4 + b, 0:TH], ones[:, 0:1].to_broadcast([P, P]),
                                   ssum[:, b * TH:(b + 1) * TH], start=True, stop=True)
                mm.then_inc(stats_done, 1)

            pe.wait_ge(ident_ready, 4)
            pe.wait_ge(x_landed, 64)
            for m in range(KT):
                if due(m - 1):
                    pe.wait_ge(x_ready, m - 1)
                for c in range(NC):
                    mm = pe.transpose(ps[:, 4 + m % 2, c * P:(c + 1) * P], xtok[:, c, m * P:(m + 1) * P], ident[:, :])
                mm.then_inc(xt_done, 1)
                if m == 0:
                    pe.wait_ge(xs_landed, 16)
                    for k in range(KT):
                        mm = pe.transpose(ps[:, 6, k * NS:(k + 1) * NS], xs_row[:, k * P:(k + 1) * P],
                                          ident[0:NS, 0:NS])
                    pe.wait_ge(frow_landed, 96)
                    pe.transpose(ps[:, 6, 128:128 + FEAT], frow[:, :], ident[0:FEAT, 0:FEAT]).then_inc(frow_done, 1)
            pe.wait_ge(crow_landed, 144)
            pe.wait_ge(feat_ready, 1)
            pe.wait_ge(xs_ready, 1)
            for half in range(2):
                for i in range(16):
                    mm = pe.transpose(ps[:, 6 + half, i * CW:(i + 1) * CW], crow[:, 16 * half + i, :],
                                      ident[0:CW, 0:CW])
                mm.then_inc(crow_done, 1)

            pe.wait_ge(const_ready, 2)
            pe.wait_ge(x_ready, 8)
            unit(Pair(J_DT), 1, h_hi, h_lo, k_ready=h_ready(0))
            stats(0)
            pe.wait_ge(dt_vec_done, 9)
            pe.wait_ge(dt_act_done, 10)
            pe.wait_ge(root_done, 1)
            for n, src in enumerate((dt_dt, dt_end.rearrange("p a b -> p (a b)"), dt_a)):
                for c in range(NC):
                    j = n * NC + c
                    mm = pe.transpose(ps[:, 4, j * HEADS:(j + 1) * HEADS], src[:, c * CH:(c + 1) * CH],
                                      ident[0:HEADS, 0:HEADS])
            mm.then_inc(dt_tr_done, 1)

            def raw_tr(g, t):
                pe.wait_ge(evac_done, Pair(group_pair(g) + t // 2).unit(t % 2, 1))
                pe.wait_ge(sraw_filled, 4 * g + t + 1)
                if t == 0:
                    if due(g):
                        pe.wait_ge(cst_evac, g)
                    pe.wait_ge(crow_done, 2)
                    pe.wait_ge(convf_ready, 2)
                    if due(g - 1):
                        pe.wait_ge(yroot_done, g - 1)
                pe.transpose(ps[0:35, 7, t * P:(t + 1) * P], raw[:, t % 2, TP:TP + 35], ident[:, :])\
                  .then_inc(cst_tr, 1)

            def gu(g, u):
                if g is not None:
                    unit(Pair(group_pair(g) + u // 2), u % 2, h_hi, h_lo, PROMPT if u < 4 else EVEN)

            def rms(g):
                if g < 0:
                    return
                pe.wait_ge(ysum_done, g + 1)
                pe.wait_ge(cst_evac, min(g + 2, GROUPS))
                pe.wait_ge(comb_done, 2 * g + 2)
                for b in range(2):
                    mm = pe.matmul(ps[:, 6 + b, 0:TH], ones[:, 0:1].to_broadcast([P, P]),
                                   ssum[:, b * TH:(b + 1) * TH], start=True, stop=True)
                mm.then_inc(rms_done, 1)

            def state_out(g):
                if g < 0:
                    return
                pe.wait_ge(hstep_done, 4 * g + 4)
                pe.wait_ge(comb_done, 2 * g + 2)
                for i in range(2):
                    mm = pe.transpose(ps[:, 5, 256 + i * N:256 + (i + 1) * N], hprev[:, 3, i * P:(i + 1) * P], ident[:, :])
                mm.then_inc(h4_tr, 1)

            def window(g, nxt):
                A = act[:, g % 2]
                gu(nxt, 0)
                pe.wait_ge(silu_done, 4 * g + 4)
                if due(2 * g):
                    pe.wait_ge(comb_done, 2 * g)
                pe.wait_ge(dt_tok_done, 1)
                for i in range(2):
                    for c in range(NC):
                        mm = pe.transpose(ps[:, 4 + i, c * P:(c + 1) * P], A[:, 2 + i, c * CH:(c + 1) * CH], ident[:, :])
                    mm.then_inc(xtr_done, 1)
                rms(g - 1)
                gu(nxt, 1)
                if due(g):
                    pe.wait_ge(yroot_done, g)
                for c in range(NC):
                    mm = pe.transpose(ps[:, 6, c * P:(c + 1) * P], A[:, 0, c * CH:(c + 1) * CH], ident[:, :])
                mm.then_inc(Btr_done, 1)
                pe.wait_ge(xdt_done, 2 * g + 1)
                for c in range(NC):
                    mm = pe.matmul(ps[:, 4, c * CH:(c + 1) * CH], A[:, 0, c * CH:(c + 1) * CH],
                                   A[:, 1, c * CH:(c + 1) * CH], start=True, stop=True)
                mm.then_inc(cb_done, 1)
                pe.wait_ge(xdt_done, 2 * g + 2)
                state_out(g - 1)
                for i in range(2):
                    mm = pe.transpose(ps[0:NS, 5, i * N:(i + 1) * N], A[:, i, S0:CONV_N:TAPS], ident[:, :])
                mm.then_inc(bc_tr, 1)
                if nxt is not None:
                    raw_tr(nxt, 0)
                gu(nxt, 2)
                for i in range(2):
                    pe.wait_ge(m_done, 4 * g + 2 * i + 2)
                    if i == 0:
                        pe.wait_ge(cbm_done, g + 1)
                    else:
                        pe.wait_ge(bc_evac, g + 1)
                        if due(g):
                            pe.wait_ge(h4_evac, g)
                    for hh in range(2):
                        for c in range(NC):
                            mm = pe.matmul(ps[hh * HD:(hh + 1) * HD, 4 + i, c * CH:(c + 1) * CH],
                                           xdt[:, c, (2 * i + hh) * HD:(2 * i + hh + 1) * HD],
                                           abc[:, hh, c * CH:(c + 1) * CH], start=True, stop=True)
                    mm.then_inc(ydiag_done, 1)
                    if nxt is not None:
                        raw_tr(nxt, 1 + i)
                    gu(nxt, 3 + i)
                pe.wait_ge(xdte_done, g + 1)
                pe.wait_ge(Btok_done, g + 1)
                if nxt is not None:
                    raw_tr(nxt, 3)
                for c in range(NC):
                    if c == 2:
                        pe.wait_ge(y1_done, 2 * g + 1)
                    mm = pe.matmul(ps[:, 6 if c < 2 else 4, (c % 2) * 256:(c % 2) * 256 + 256],
                                   Btok[:, c, :], xdt[:, c, :], start=True, stop=True)
                    mm.then_inc(st_done, 1)
                gu(nxt, 5)
                pe.wait_ge(y1_done, 2 * g + 2)
                for i in range(2):
                    for c in range(1, NC):
                        if i == 0:
                            pe.wait_ge(hstep_done, 4 * g + c)
                        mm = pe.matmul(ps[:, 5 + i, c * CH:(c + 1) * CH], hprev[:, c - 1, i * P:(i + 1) * P],
                                       A[:, 1, c * CH:(c + 1) * CH], start=True, stop=True)
                    mm.then_inc(yoff_done, 1)

            for u in range(6):
                gu(0, u)
                if u in (1, 2, 3):
                    raw_tr(0, u - 1)
                if u == 4:
                    raw_tr(0, 3)
            for g in range(5):
                window(g, g + 1)

            def y_ready(first):
                def ready(k):
                    pe.wait_ge(y_hi_done, 2 * first + k + 1)
                    pe.wait_ge(y_lo_done, 2 * first + k + 1)
                return ready

            def out_product(J, k_ready, before=None):
                for i in range(4):
                    for half in range(2):
                        unit(Pair(J + i), half, a_hi, a_lo, k_ready=k_ready if i == half == 0 else None)
                        if before and i == half == 0:
                            before()

            out_product(J_OUT0, y_ready(0))
            window(5, 6)
            window(6, 7)
            window(7, None)
            rms(7)
            state_out(7)
            out_product(J_OUT1, y_ready(4))

            def out_tr(m):
                pe.wait_ge(xg_done, m + 1)
                if due(m - 1):
                    pe.wait_ge(ty_evac, m - 1)
                if m == 0:
                    pe.wait_ge(root_done, 4)
                for c in range(NC):
                    mm = pe.transpose(ps[:, 4 + m % 2, c * P:(c + 1) * P], xg[:, m % 2, c * CH:(c + 1) * CH], ident[:, :])
                mm.then_inc(ty_done, 1)
                pe.transpose(ps[0:NS, 6 + m // 4, (m % 4) * P:(m % 4 + 1) * P], xg[:, m % 2, TP:T], ident[:, :])\
                  .then_inc(ty_done, 1)

            def mlp(n, J):
                def chunk(c, first, final=False):
                    for i in range(4):
                        for half in range(2):
                            unit(Pair(J + i, c * 4), half, h_hi, h_lo,
                                 k_ready=h_ready(n) if first and i == half == 0 else None)
                            if first and i == half == 0:
                                stats(n)
                    for i in range(4):
                        for half in range(2):
                            done = 0 if n == 1 else 48

                            def ready(k):
                                pe.wait_ge(a_hi_done, c * 8 + (done + k + 1))
                                pe.wait_ge(a_lo_done, c * 8 + (done + k + 1))

                            unit(Pair(J + 4 + i, c * 4), half, a_hi, a_lo,
                                 k_ready=ready if i == half == 0 else None)
                            if final and n == 3 and i + half:
                                out_tr(2 * i + half - 1)
                chunk(0, True)
                with pe.Fori(1, CHUNKS - 1) as c:
                    chunk(c, False)
                chunk(CHUNKS - 1, False, final=True)

            mlp(1, J_MLP0)

            for i in range(8):
                for half in range(2):
                    j = 2 * i + half
                    unit(Pair(J_V + i), half, h_hi, h_lo, k_ready=h_ready(2) if j == 0 else None)
                    if j == 0:
                        stats(2)
                    if j == 1:
                        pe.wait_ge(mix_landed, 16)
                        for g in range(8):
                            mm = pe.transpose(ps[:, 6 + g // 4, (g % 4) * P:(g % 4 + 1) * P], wmix[:, g, :], ident[:, :])
                        mm.then_inc(mixT_done, 1)
                    if j >= 1:
                        tile = j - 1
                        pe.wait_ge(gelu_done, tile + 1)
                        if due(tile - 1):
                            pe.wait_ge(vtok_done, tile - 1)
                        pe.wait_ge(root_done, 3)
                        for c in range(NC):
                            mm = pe.transpose(ps[:, 4 + tile % 2, c * P:(c + 1) * P],
                                              gv[:, tile % 2, c * CH:(c + 1) * CH], ident[:, :])
                        mm.then_inc(v_tr, 1)
            pe.wait_ge(gelu_done, 16)
            pe.wait_ge(vtok_done, 14)
            for c in range(NC):
                mm = pe.transpose(ps[:, 5, c * P:(c + 1) * P], gv[:, 1, c * CH:(c + 1) * CH], ident[:, :])
            mm.then_inc(v_tr, 1)

            def v_stats():
                pe.wait_ge(vsum_done, 15)
                pe.wait_ge(vtok_done, 16)
                for c in range(NC):
                    pe.matmul(ps[:, 4, c:c + 1], ssum[:, c * CH:(c + 1) * CH], ones[:, 0:1], start=True, stop=True)
                pe.matmul(ps[:, 4, 8:8 + NS], ones[:, 0:1].to_broadcast([P, P]), ssum[:, TP:T],
                          start=True, stop=True).then_inc(vstat_done, 1)

            def v_rows(n):
                pe.wait_ge(vsn_done, 2)
                if due(n - 1):
                    pe.wait_ge(vs_evac, n - 1)
                for i in range(4):
                    mm = pe.transpose(ps[0:NS, 6 + n % 2, i * P:(i + 1) * P], vsmp[:, 4 * n + i, :], ident[:, :])
                mm.then_inc(vs_tr, 1)

            def u_half(first, J):
                for i in range(4):
                    for half in range(2):
                        j = first + 2 * i + half
                        unit(Pair(J + i), half, h_hi, h_lo)
                        if j == 0:
                            v_stats()
                            pe.wait_ge(wmask_done, 2)
                            pe.wait_ge(vrec_done, 2)
                            pe.wait_ge(vscaled, 4)
                        if due(j - 1):
                            pe.wait_ge(s_done, j - 1)
                        for c in range(NC):
                            mm = pe.matmul(ps[:, 4 + j % 2, c * CH:(c + 1) * CH], vtok[:, c, j * P:(j + 1) * P],
                                           wmixT[:, j // 2, :], start=True, stop=True)
                        mm.then_inc(mixed, 1)
                        if 1 <= j < 5:
                            v_rows(j - 1)

            def gated_ready(first):
                def ready(k):
                    pe.wait_ge(a_hi_done, 32 + first + k + 1)
                    pe.wait_ge(a_lo_done, 32 + first + k + 1)
                return ready

            u_half(0, J_U0)
            out_product(J_CMO0, gated_ready(0))
            u_half(8, J_U1)
            out_product(J_CMO1, gated_ready(8))
            mlp(3, J_MLP1)

            out_tr(KT - 1)
            pe.wait_ge(ty_evac, 8)
            pe.wait_ge(ssum_added, 35)
            for c in range(NC):
                pe.matmul(ps[:, 4, c:c + 1], ssum[:, c * CH:(c + 1) * CH], ones[:, 0:1], start=True, stop=True)
            pe.matmul(ps[0:NS, 5, 0:1], ssum[:, TP:T], ones[:, 0:1], start=True, stop=True).then_inc(fin_stat, 1)

        @block.scalar
        def _(act_e):
            def split_w(pair):
                act_e.wait_ge(w_landed[pair.slot], pair.use(1) * 16)
                if due(c_columns(pair)):
                    act_e.wait_ge(c_landed, c_columns(pair))
                if due(pair.times(2, -3)):
                    act_e.wait_ge(unit_done, pair.times(2, -3))
                w = slice(0, P if pair.s == J_DT and isinstance(pair.loop, int) else 256)
                nc.scalar.activation(w_hi[:, pair.slot, :, w], w32[:, pair.slot, :, w], ACT.Copy)\
                  .then_inc(w_hi_done, 1)

            def square(n, m, x_final):
                x_final(m)
                if m == 0:
                    if due(n):
                        act_e.wait_ge(r_ready, n)
                    if n == 1:
                        act_e.wait_ge(y_lo_done, 16)
                    if n == 3:
                        act_e.wait_ge(vrec_done, 2)
                        act_e.wait_ge(a_lo_done, 48)
                    dst = ssum[:, :]
                else:
                    if due(7 * n + m - 2):
                        act_e.wait_ge(ssum_added, 7 * n + m - 2)
                    dst = sq[:, m % 2, :]
                nc.scalar.activation(dst, xT[:, m, :], ACT.Square).then_inc(sq_ready, 1)

            def make_h(n, m, gain, x_final, read_out):
                x_final(m)
                if due(read_out):
                    act_e.wait_ge(unit_done, read_out)
                nc.scalar.activation(h_hi[:, m, :], xT[:, m, :], ACT.Copy, scale=feat[:, gain + m:gain + m + 1])\
                  .then_inc(h_hi_ready, 1)
                square(n, m, x_final)

            def root(n):
                act_e.wait_ge(stats_done, n + 1)
                nc.scalar.activation(halves(ssum[:, :]), ps[:, 4:6, 0:TH], ACT.Sqrt, bias=eps[:, 0:1], scale=1.0 / D)\
                  .then_inc(root_done, 1)

            act_e.dma_start(xs_row[:, :], x_sample.rearrange("b s d -> (b s) d")).then_inc(xs_landed, 16)
            r0 = 0
            for src in (norm_mix_g.rearrange("l (t c) -> (l t) c", c=P), norm_mlp_g.rearrange("l (t c) -> (l t) c", c=P),
                        norm_final_g.rearrange("(t c) -> t c", c=P), ssd_norm_g[0].rearrange("(t c) -> t c", c=P),
                        cm_b_in[0].rearrange("(t c) -> t c", c=P), cm_v_norm_g[0].rearrange("(t c) -> t c", c=P)):
                act_e.dma_start(frow[r0:r0 + src.shape[0], :], src).then_inc(frow_landed, 16)
                r0 += src.shape[0]
            r0 = 0
            by_group = crow.rearrange("r (g t) c -> r g t c", t=4)
            for src in (ssd_conv_w[0], ssd_conv_b[0:1], state_conv[0].rearrange("b k c -> (b k) c")):
                n = src.shape[0]
                for i in range(2):
                    act_e.dma_start(by_group[r0:r0 + n, :, i, :],
                                    src[:, DI + i * GROUPS * N:DI + (i + 1) * GROUPS * N].rearrange("r (g c) -> r g c", c=P))\
                         .then_inc(crow_landed, 16)
                act_e.dma_start(by_group[r0:r0 + n, :, 2:4, :],
                                src[:, 0:DI].rearrange("r (g t c) -> r g t c", t=2, c=P)).then_inc(crow_landed, 16)
                r0 += n
            act_e.dma_start(conv_sample[0, :, 0:2, :], state_conv[0, :, 1:3, :]).then_inc(conv_old, 16)

            def x_prologue(m):
                act_e.wait_ge(x_ready, m + 1)
                act_e.wait_ge(xs_ready, 1)

            act_e.wait_ge(feat_ready, 1)
            for m in range(KT):
                make_h(0, m, G_MIX, x_prologue, 0)
            split_w(Pair(J_DT))
            split_w(Pair(1))
            act_e.wait_ge(const_ready, 2)
            root(0)

            for i, src in ((0, ssd_dt_bias), (1, ssd_a_log), (2, ssd_d)):
                act_e.wait_ge(crow_done, 2)
                act_e.dma_start(dt_par[:, i:i + 1], src[0].rearrange("(h o) -> h o", o=1)).then_inc(par_landed, 16)
            act_e.wait_ge(par_landed, 48)
            nc.scalar.activation(dt_par[:, 1:2], dt_par[:, 1:2], ACT.Exp).then_inc(dt_act_done, 1)
            act_e.wait_ge(dt_vec_done, 1)
            nc.scalar.activation(dt_e[:, :], dt_v[:, :], ACT.Abs).then_inc(dt_act_done, 1)
            act_e.wait_ge(dt_act_done, 2)
            nc.scalar.activation(dt_e[:, :], dt_e[:, :], ACT.Exp, scale=-1.0).then_inc(dt_act_done, 1)
            act_e.wait_ge(dt_act_done, 3)
            nc.scalar.activation(dt_e[:, :], dt_e[:, :], ACT.Ln, bias=ones[0:HEADS, 0:1]).then_inc(dt_act_done, 1)
            for c in range(NC):
                act_e.wait_ge(dt_vec_done, 5 + c)
                nc.scalar.activation(dt_end[:, c, :], dt_a[:, c * CH:(c + 1) * CH], ACT.Exp,
                                     bias=dt_a[:, (c + 1) * CH - 1:(c + 1) * CH], scale=-1.0).then_inc(dt_act_done, 1)
            nc.scalar.activation(dt_small[:, 8:16], dt_v[:, TP:T], ACT.Exp).then_inc(dt_act_done, 1)
            nc.scalar.activation(dt_small[:, 20:24], dt_a[:, CH - 1:TP:CH], ACT.Exp).then_inc(dt_act_done, 1)
            act_e.wait_ge(dt_vec_done, 9)
            act_e.wait_ge(dt_act_done, 10)
            act_e.dma_start(scr_a, dt_a[:, 0:TP]).then_inc(scr_a_done, 16)
            act_e.dma_start(scr_s, dt_small[:, :]).then_inc(scr_s_done, 16)
            act_e.wait_ge(scr_s_done, 16)
            for hh in range(2):
                act_e.dma_start(dtf[hh * HD:(hh + 1) * HD, :, :], scr_s[hh:HEADS:2, 0:20].partition_broadcast(HD))\
                     .then_inc(dtf_landed, 16)
            act_e.dma_start(cdec[:, :, :], scr_s[:, 20:24].partition_broadcast(P)).then_inc(cdec_landed, 16)
            act_e.wait_ge(scr_a_done, 16)

            def fill(g, t):
                k = 4 * g + t
                if due(k - 1):
                    act_e.wait_ge(tap0_done, k - 1)
                if due(3 * (k - 1)):
                    act_e.wait_ge(tap_done, 3 * (k - 1))
                if due(k - 1):
                    act_e.wait_ge(cst_tr, k - 1)
                if k < 2:
                    act_e.wait_ge(convf_ready, 2)
                    act_e.wait_ge(raw_zeroed, 1)
                nc.scalar.activation(raw[:, t % 2, S0:RAW].rearrange("p (b k) -> p b k", k=TAPS)[:, :, 0:3],
                                     convf[:, k, 5:CW].rearrange("p (b k) -> p b k", k=3), ACT.Copy)\
                  .then_inc(sraw_filled, 1)

            def tap0(g, t):
                k = 4 * g + t
                act_e.wait_ge(evac_done, Pair(group_pair(g) + t // 2).unit(t % 2, 1))
                act_e.wait_ge(sraw_filled, k + 1)
                if due(2 * g - 2):
                    act_e.wait_ge(yoff_done, 2 * g - 2)
                if due(2 * g - 2):
                    act_e.wait_ge(comb_done, 2 * g - 2)
                if due(g - 1):
                    act_e.wait_ge(xdts_done, g - 1)
                nc.scalar.activation(act[:, g % 2, t, :], raw[:, t % 2, 0:CONV_N], ACT.Identity,
                                     bias=convf[:, k, 4:5], scale=convf[:, k, 0:1]).then_inc(tap0_done, 1)

            def silu(g, t):
                act_e.wait_ge(tap_done, 3 * (4 * g + t + 1))
                nc.scalar.activation(act[:, g % 2, t, :], act[:, g % 2, t, :], ACT.Silu).then_inc(silu_done, 1)

            def silu_z(g, i):
                act_e.wait_ge(evac_done, Pair(group_pair(g) + 2).unit(i, 1))
                nc.scalar.activation(zs[:, g % 2, i, :], zs[:, g % 2, i, :], ACT.Silu).then_inc(z_silu_done, 1)

            def cst(g):
                act_e.wait_ge(cst_tr, 4 * g + 4)
                if due(64 * g):
                    act_e.wait_ge(cst_out, 64 * g)
                nc.scalar.activation(cstage[:, :, :], ps[0:35, 7, :].rearrange("p (t c) -> p t c", c=P), ACT.Copy)\
                  .then_inc(cst_evac, 1)

            def y_squares(g):
                if g < 0:
                    return
                for i, dst in ((0, ssum[:, :]), (1, sq[:, 0, :])):
                    act_e.wait_ge(comb_done, 2 * g + i + 1)
                    if due(g):
                        act_e.wait_ge(ysum_done, g)
                    if due(2 * g):
                        act_e.wait_ge(ynorm_done, 2 * g)
                    act_e.wait_ge(r_ready, 1)
                    nc.scalar.activation(dst, work[:, i, :], ACT.Square).then_inc(ysq_done, 1)

            def y_root(g):
                if g < 0:
                    return
                act_e.wait_ge(rms_done, g + 1)
                nc.scalar.activation(halves(ssum[:, :]), ps[:, 6:8, 0:TH], ACT.Sqrt, bias=eps[:, 0:1], scale=1.0 / 256)\
                  .then_inc(yroot_done, 1)

            def y_high(g):
                if g < 0:
                    return
                for i in range(2):
                    act_e.wait_ge(ynorm_done, 2 * g + i + 1)
                    if g >= 4:
                        act_e.wait_ge(unit_done, Pair(J_OUT0 + 3).unit(1, 1))
                    nc.scalar.activation(a_hi[:, (2 * g + i) % 8, :], work[:, i, :], ACT.Copy).then_inc(y_hi_done, 1)

            def state_evac(g):
                if g < 0:
                    return
                act_e.wait_ge(h4_tr, g + 1)
                if due(32 * g):
                    act_e.wait_ge(ssm_out, 32 * g)
                nc.scalar.activation(ssm_stage[:, :, :], ps[:, 5, 256:512].rearrange("p (i n) -> p i n", i=2), ACT.Copy)\
                  .then_inc(h4_evac, 1)

            def abc_load(g, i):
                if due(2 * g):
                    act_e.wait_ge(comb_done, 2 * g)
                if due(2 * g + i):
                    act_e.wait_ge(ydiag_done, 2 * g + i)
                if g == 0:
                    act_e.wait_ge(dt_tok_done, 1)
                    act_e.wait_ge(dtf_landed, 32)
                act_e.dma_start(abc[:, :, :], scr_a[4 * g + 2 * i:4 * g + 2 * i + 2, :].partition_broadcast(P))\
                     .then_inc(abc_landed, 16)

            def exp_m(g, i):
                for hh in range(2):
                    n = 4 * g + 2 * i + hh
                    act_e.wait_ge(seg_done, n + 1)
                    nc.scalar.activation(abc[:, hh, :], abc[:, hh, :], ACT.Exp).then_inc(exp_done, 1)

            def ef(g):
                act_e.wait_ge(ydiag_done, 2 * g + 2)
                for i in range(2):
                    for hh in range(2):
                        act_e.dma_start(abc[hh * HD:(hh + 1) * HD, i, :],
                                        scr_a[4 * g + 2 * i + hh, :].partition_broadcast(HD)).then_inc(ef_landed, 16)

            def ef_exp(g):
                act_e.wait_ge(ef_landed, 64 * (g + 1))
                for i in range(2):
                    nc.scalar.activation(abc[:, i, :], abc[:, i, :], ACT.Exp).then_inc(ef_done, 1)

            def window(g, nxt):
                J = None if nxt is None else group_pair(nxt)
                if J is not None:
                    split_w(Pair(J + 1))
                abc_load(g, 0)
                y_squares(g - 1)
                if J is not None:
                    fill(nxt, 0)
                    tap0(nxt, 0)
                    fill(nxt, 1)
                y_root(g - 1)
                exp_m(g, 0)
                act_e.wait_ge(Btr_done, g + 1)
                if due(4 * g):
                    act_e.wait_ge(st_done, 4 * g)
                nc.scalar.activation(Btok[:, :, :], ps[:, 6, :].rearrange("p (c n) -> p c n", n=N), ACT.Copy)\
                  .then_inc(Btok_done, 1)
                y_high(g - 1)
                act_e.wait_ge(bc_tr, g + 1)
                if due(16 * g):
                    act_e.wait_ge(bc_out, 16 * g)
                nc.scalar.activation(bcrow[:, :], ps[0:NS, 5, 0:2 * N], ACT.Copy).then_inc(bc_evac, 1)
                state_evac(g - 1)
                if J is not None:
                    tap0(nxt, 1)
                    fill(nxt, 2)
                    split_w(Pair(J + 2))
                    silu(nxt, 0)
                    silu(nxt, 1)
                    tap0(nxt, 2)
                    fill(nxt, 3)
                abc_load(g, 1)
                exp_m(g, 1)
                if J is not None:
                    tap0(nxt, 3)
                    split_w(Pair(J + 3))
                    silu(nxt, 2)
                    silu(nxt, 3)
                ef(g)
                if J is not None:
                    cst(nxt)
                    silu_z(nxt, 0)
                ef_exp(g)
                if J is not None:
                    silu_z(nxt, 1)

            fill(0, 0)
            fill(0, 1)
            tap0(0, 0)
            split_w(Pair(2))
            tap0(0, 1)
            fill(0, 2)
            silu(0, 0)
            silu(0, 1)
            tap0(0, 2)
            fill(0, 3)
            split_w(Pair(3))
            tap0(0, 3)
            silu(0, 2)
            silu(0, 3)
            cst(0)
            split_w(Pair(4))
            silu_z(0, 0)
            silu_z(0, 1)
            for g in range(5):
                window(g, g + 1)
            for i in range(4):
                split_w(Pair(J_OUT0 + i + 1))
            window(5, 6)
            window(6, 7)
            window(7, None)
            y_squares(7)
            y_root(7)
            y_high(7)
            state_evac(7)

            def x_after(pair0):
                def ready(m):
                    act_e.wait_ge(evac_done, Pair(pair0.s + m // 2, pair0.loop).unit(m % 2, 1))
                return ready

            def out_with_h(n, J, gain, read_out):
                for i in range(4):
                    split_w(Pair(J + i + 1))
                    for half in range(2):
                        make_h(n, 2 * i + half, gain, x_after(Pair(J)), read_out)

            out_with_h(1, J_OUT1, G_MLP, Pair(J_OUT1 - 1).unit(1, 1))

            def mlp(n, J, last):
                base = 0 if n == 1 else 48

                def chunk(c, first, final):
                    for i in range(4):
                        split_w(Pair(J + i + 1, c * 4))
                        if first and i == 0:
                            root(n)
                        for half in range(2):
                            j = 2 * i + half
                            act_e.wait_ge(a32_done, c * 8 + (base + j + 1))
                            if first and i == half == 0:
                                act_e.wait_ge(unit_done, Pair(J - 1).unit(1, 1))
                            elif not first:
                                act_e.wait_ge(unit_done, Pair(J + i, c * 4).unit(half, 0))
                            nc.scalar.activation(a_hi[:, j, :], work[:, half, :], ACT.Copy).then_inc(a_hi_done, 1)
                    for i in range(4):
                        if not (final and last and i == 3):
                            split_w(Pair(J + 4 + i + 1, c * 4))
                        if final:
                            for half in range(2):
                                m = 2 * i + half
                                up_done = Pair(J + 3, c * 4).unit(1, 1)
                                if last:
                                    final_tile(m)
                                else:
                                    make_h(n + 1, m, G_MIX + KT, x_after(Pair(J + 4, c * 4)), up_done)

                def final_tile(m):
                    square(4, m, x_after(Pair(J + 4 + 8 * (CHUNKS - 1))))

                chunk(0, True, False)
                with act_e.Fori(1, CHUNKS - 1) as c:
                    chunk(c, False, False)
                chunk(CHUNKS - 1, False, True)

            mlp(1, J_MLP0, False)

            act_e.wait_ge(sstored, 16 * 32)
            act_e.wait_ge(ssm_out, 32 * 8)
            act_e.wait_ge(cst_out, 64 * 8)
            for i in range(8):
                split_w(Pair(J_V + i + 1))
                if i == 0:
                    root(2)
                for half in range(2):
                    j = 2 * i + half
                    act_e.wait_ge(evac_done, Pair(J_V + i).unit(half, 1))
                    if due(j - 1):
                        act_e.wait_ge(v_tr, j - 1)
                    if due(j - 1):
                        act_e.wait_ge(vsmp_done, j - 1)
                    nc.scalar.activation(gv[:, j % 2, :], work[:, j % 2, :], ACT.Gelu,
                                         bias=feat[:, B_CM + 16 + j:B_CM + 17 + j]).then_inc(gelu_done, 1)
                    act_e.wait_ge(gelu_done, j + 1)
                    if j == 0:
                        act_e.wait_ge(r_ready, 3)
                    else:
                        if due(j - 2):
                            act_e.wait_ge(vsum_done, j - 2)
                    nc.scalar.activation(ssum[:, :] if j == 0 else sq[:, j % 2, :], gv[:, j % 2, :], ACT.Square)\
                      .then_inc(vsq_done, 1)

            def u_half(first, J):
                for i in range(4):
                    split_w(Pair(J + i + 1))
                    for half in range(2):
                        j = first + 2 * i + half
                        act_e.wait_ge(evac_done, Pair(J + i).unit(half, 1))
                        nc.scalar.activation(work[:, j % 2, :], work[:, j % 2, :], ACT.Gelu,
                                             bias=feat[:, B_CM + j:B_CM + 1 + j]).then_inc(gelu_done, 1)
                        if j == 0:
                            act_e.wait_ge(vstat_done, 1)
                            nc.scalar.activation(r_tok[:, 0:NC], ps[:, 4, 0:NC], ACT.Sqrt, bias=eps[:, 0:1],
                                                 scale=1.0 / CMW).then_inc(vroot_done, 1)
                            nc.scalar.activation(r_smp[:, :], ps[:, 4, 8:8 + NS], ACT.Sqrt, bias=eps[:, 0:1],
                                                 scale=1.0 / CMW).then_inc(vroot_done, 1)
                        act_e.wait_ge(a32_done, 32 + j + 1)
                        act_e.wait_ge(unit_done, Pair(J_MLP0 + 31).unit(1, 1) if first == 0 else Pair(J_CMO0 + 3).unit(1, 1))
                        nc.scalar.activation(a_hi[:, j % 8, :], sq[:, j % 2, :], ACT.Copy).then_inc(a_hi_done, 1)

            u_half(0, J_U0)
            for i in range(4):
                split_w(Pair(J_CMO0 + i + 1))
            u_half(8, J_U1)
            out_with_h(3, J_CMO1, G_MLP + KT, Pair(J_CMO1 - 1).unit(1, 1))
            mlp(3, J_MLP1, True)
            act_e.wait_ge(fin_stat, 1)
            nc.scalar.activation(r_fin[:, 0:NC], ps[:, 4, 0:NC], ACT.Sqrt, bias=eps[:, 0:1], scale=1.0 / D)\
              .then_inc(fin_root, 1)
            nc.scalar.activation(r_fin[0:NS, NC:NC + 1], ps[0:NS, 5, 0:1], ACT.Sqrt, bias=eps[0:NS, 0:1], scale=1.0 / D)\
              .then_inc(fin_root, 1)

        @block.gpsimd
        def _(pool):
            nc.gpsimd.memset(ident[:, :], 1.0).then_inc(ident_ready, 1)
            nc.gpsimd.memset(causal[:, :], 1.0).then_inc(ident_ready, 1)
            pool.wait_ge(ident_ready, 2)
            nc.gpsimd.affine_select(out=ident[:, :], in_=ident[:, :], compare_op=ALU.is_equal, fill=0.0, base=0,
                                    pattern=[[-1, P]], channel_multiplier=1).then_inc(ident_ready, 1)
            nc.gpsimd.affine_select(out=causal[:, :], in_=causal[:, :], compare_op=ALU.is_ge, fill=0.0, base=0,
                                    pattern=[[1, P]], channel_multiplier=-1).then_inc(ident_ready, 1)
            nc.gpsimd.memset(w32[:, 0, :, HEADS:P], 0.0).then_inc(w_cleared, 1)
            nc.gpsimd.memset(ones[:, :], 1.0).then_inc(const_ready, 1)
            nc.gpsimd.memset(eps[:, :], EPS).then_inc(const_ready, 1)

            def add_squares(n):
                for m in range(1, KT):
                    pool.wait_ge(sq_ready, 8 * n + m + 1)
                    if due(7 * n + m - 1):
                        pool.wait_ge(ssum_added, 7 * n + m - 1)
                    nc.gpsimd.tensor_tensor(ssum[:, :], ssum[:, :], sq[:, m % 2, :], ALU.add).then_inc(ssum_added, 1)

            add_squares(0)
            pool.wait_ge(crow_done, 2)
            pool.wait_ge(x_ready, 8)
            pool.wait_ge(xt_done, 8)
            nc.gpsimd.memset(dt_one[:, :], 1.0).then_inc(const_ready, 1)
            nc.gpsimd.memset(dt_small[:, :], 0.0).then_inc(const_ready, 1)
            nc.gpsimd.memset(raw[:, :, 0:TAPS - 1], 0.0).then_inc(raw_zeroed, 1)

            def y_sum(g):
                if g < 0:
                    return
                pool.wait_ge(ysq_done, 2 * g + 2)
                nc.gpsimd.tensor_tensor(ssum[:, :], ssum[:, :], sq[:, 0, :], ALU.add).then_inc(ysum_done, 1)

            def store_state(g):
                if g < 0:
                    return
                pool.wait_ge(h4_evac, g + 1)
                for i in range(2):
                    h0 = 4 * g + 2 * i
                    pool.dma_start(ssm_prompt[0, 0, h0:h0 + 2].rearrange("h p n -> (h p) n"), ssm_stage[:, i, :])\
                        .then_inc(ssm_out, 16)

            def store_conv(g):
                pool.wait_ge(cst_evac, g + 1)
                x0, b0 = 2 * g * P, DI + g * N
                for row, dst in ((slice(0, 3), conv_prompt[0, 0]), (slice(6, 35, 4), conv_sample[0, :, 2])):
                    pool.dma_start(dst[:, x0:x0 + 2 * P], cstage[row, 2:4, :]).then_inc(cst_out, 16)
                    pool.dma_start(dst[:, DI:DI + 2 * GROUPS * N].rearrange("r (b c) -> r b c", b=2)[:, :, g * N:(g + 1) * N],
                                   cstage[row, 0:2, :]).then_inc(cst_out, 16)

            def window(g, nxt):
                y_sum(g - 1)
                pool.wait_ge(bc_evac, g + 1)
                pool.dma_start(scr_bc[g], bcrow[:, :]).then_inc(bc_out, 16)
                store_state(g - 1)
                pool.wait_ge(bc_out, 16 * (g + 1))
                pool.wait_ge(xdts_done, g + 1)
                for hb in range(2):
                    if due(4 * g + 2 * hb):
                        pool.wait_ge(smul_done, 4 * g + 2 * hb)
                    if due(4 * g + 2 * hb):
                        pool.wait_ge(outer_done, 4 * g + 2 * hb)
                    pool.dma_start(bcs[:, :, :], scr_bc[g, 4 * hb:4 * hb + 4, :].partition_broadcast(P))\
                        .then_inc(bcs_landed, 16)
                    for i in range(2):
                        n = 4 * g + 2 * hb + i
                        h0 = 4 * g + 2 * i
                        b = slice(4 * hb, 4 * hb + 4)
                        if due(n):
                            pool.wait_ge(smul_done, n)
                        if due(16 * n):
                            pool.wait_ge(sstored, 16 * n)
                        pool.dma_start(hst[:, :, :], state_ssm[0, b, h0:h0 + 2].rearrange("b h p n -> (h p) b n"))\
                            .then_inc(hst_landed, 16)
                        if i == 0:
                            pool.wait_ge(bcs_landed, 16 * (2 * g + hb + 1))
                        if due(n):
                            pool.wait_ge(snew_done, n)
                        nc.gpsimd.tensor_tensor(outer[:, :, :], bcs[:, :, 0:N],
                                                xdts[:, i, b].unsqueeze(2).broadcast_to([P, 4, N]), ALU.mult)\
                          .then_inc(outer_done, 1)
                        pool.wait_ge(hst_landed, 16 * (n + 1))
                        nc.gpsimd.tensor_tensor(hst[:, :, :], hst[:, :, :],
                                                dtf[:, 2 * g + i, 8 + 4 * hb:12 + 4 * hb].unsqueeze(2).broadcast_to([P, 4, N]),
                                                ALU.mult).then_inc(decay_done, 1)
                        pool.wait_ge(outer_done, n + 1)
                        pool.wait_ge(decay_done, n + 1)
                        nc.gpsimd.tensor_tensor(hst[:, :, :], hst[:, :, :], outer[:, :, :], ALU.add)\
                          .then_inc(snew_done, 1)
                        pool.wait_ge(snew_done, n + 1)
                        pool.dma_start(ssm_sample[0, b, h0:h0 + 2].rearrange("b h p n -> (h p) b n"), hst[:, :, :])\
                            .then_inc(sstored, 16)
                if nxt is not None:
                    store_conv(nxt)

            store_conv(0)
            for g in range(7):
                window(g, g + 1)
            window(7, None)
            y_sum(7)
            store_state(7)
            add_squares(1)
            add_squares(2)
            pool.wait_ge(sq_ready, 17)
            pool.wait_ge(sstored, 16 * 32)
            pool.wait_ge(ssm_out, 32 * 8)
            pool.wait_ge(cst_out, 64 * 8)
            pool.dma_start(wmix[:, :, :], cm_w_s[0].rearrange("g t s -> t g s")).then_inc(mix_landed, 16)
            pool.dma_start(bmix[:, :, :], cm_b_s[0].partition_broadcast(P)).then_inc(b_landed, 16)
            pool.dma_start(w00[:, :, :], cm_w_s[0, :, 0, 0:2].partition_broadcast(P)).then_inc(b_landed, 16)
            for j in range(16):
                pool.wait_ge(gelu_done, j + 1)
                nc.gpsimd.tensor_copy(vsmp[:, j, :], gv[:, j % 2, TP:T]).then_inc(vsmp_done, 1)
                if j:
                    pool.wait_ge(vsq_done, j + 1)
                    if due(j - 1):
                        pool.wait_ge(vsum_done, j - 1)
                    nc.gpsimd.tensor_tensor(ssum[:, :], ssum[:, :], sq[:, j % 2, :], ALU.add).then_inc(vsum_done, 1)
            for n in range(4):
                pool.wait_ge(vs_evac, n + 1)
                pool.dma_start(cm_v_sample[0, :, 0, n * 512:(n + 1) * 512], vs_row[:, :, :].rearrange("p a b -> p (a b)"))\
                    .then_inc(vs_out, 16)
            add_squares(3)
            add_squares(4)
            pool.wait_ge(out_done, 80)
            pool.wait_ge(conv_old, 16)
            pool.wait_ge(cst_out, 64 * 8)
            pool.wait_ge(ssm_out, 32 * 8)
            pool.wait_ge(sstored, 16 * 32)
            pool.wait_ge(vs_out, 64)

        @block.vector
        def _(dve):
            def split_w(pair):
                dve.wait_ge(w_hi_done, pair.times(1, 1))
                dve.wait_ge(w_landed[pair.slot], pair.use(1) * 16)
                if due(c_columns(pair)):
                    dve.wait_ge(c_landed, c_columns(pair))
                if due(pair.times(2, -3)):
                    dve.wait_ge(unit_done, pair.times(2, -3))
                w = slice(0, P if pair.s == J_DT and isinstance(pair.loop, int) else 256)
                nc.vector.tensor_tensor(w_lo[:, pair.slot, :, w], w32[:, pair.slot, :, w],
                                        w_hi[:, pair.slot, :, w].bitcast(F32), ALU.subtract).then_inc(w_lo_done, 1)

            def evac_scaled(pair, half, dst, n=HEADS * 4):
                dve.wait_ge(unit_done, pair.unit(half, 1))
                nc.vector.tensor_tensor(halves(dst), psum_tok(1 - half)[0:n], halves(rstd[0:n, :]), ALU.mult)\
                  .then_inc(evac_done, 1)

            def evac_added(pair, half, m):
                dve.wait_ge(unit_done, pair.unit(half, 1))
                nc.vector.tensor_tensor(halves(xT[:, m, :]), psum_tok(1 - half), halves(xT[:, m, :]), ALU.add)\
                  .then_inc(evac_done, 1)

            def h_low(n, m, gain):
                dve.wait_ge(h_hi_ready, 8 * n + m + 1)
                nc.vector.scalar_tensor_tensor(out=h_lo[:, m, :], in0=xT[:, m, :], scalar=feat[:, gain + m:gain + m + 1],
                                               in1=h_hi[:, m, :].bitcast(F32), op0=ALU.mult, op1=ALU.subtract)\
                  .then_inc(h_lo_ready, 1)

            def inv_rms(n):
                dve.wait_ge(root_done, n + 1)
                nc.vector.reciprocal(rstd[:, :], ssum[:, :]).then_inc(r_ready, 1)
                dve.wait_ge(r_ready, n + 1)

            for m in range(KT):
                dve.wait_ge(xt_done, m + 1)
                nc.vector.tensor_copy(xT[:, m, 0:TP], ps[:, 4 + m % 2, :]).then_inc(x_ready, 1)
                if m == 0:
                    dve.wait_ge(frow_done, 1)
                    nc.vector.tensor_copy(xT[:, :, TP:T], ps[:, 6, 0:KT * NS].rearrange("p (k b) -> p k b", k=KT))\
                      .then_inc(xs_ready, 1)
                    nc.vector.tensor_copy(feat[:, :], ps[:, 6, 128:128 + FEAT]).then_inc(feat_ready, 1)
                    dve.wait_ge(feat_ready, 1)
                    dve.wait_ge(xs_ready, 1)
                if m:
                    h_low(0, m - 1, G_MIX)
            h_low(0, KT - 1, G_MIX)
            split_w(Pair(J_DT))
            split_w(Pair(1))
            for half in range(2):
                dve.wait_ge(crow_done, half + 1)
                nc.vector.tensor_copy(convf[:, 16 * half:16 * half + 16, :],
                                      ps[:, 6 + half, 0:16 * CW].rearrange("p (t c) -> p t c", c=CW))\
                  .then_inc(convf_ready, 1)
            inv_rms(0)

            evac_scaled(Pair(J_DT), 1, dt_v[:, :], HEADS)
            dve.wait_ge(evac_done, 1)
            dve.wait_ge(par_landed, 48)
            dve.wait_ge(const_ready, 4)
            nc.vector.tensor_scalar(dt_v[:, :], dt_v[:, :], dt_par[:, 0:1], None, ALU.add).then_inc(dt_vec_done, 1)
            nc.vector.tensor_copy(dt_small[:, 16:17], dt_par[:, 2:3]).then_inc(dt_vec_done, 1)
            dve.wait_ge(dt_act_done, 4)
            dve.wait_ge(dt_vec_done, 2)
            nc.vector.scalar_tensor_tensor(out=dt_dt[:, :], in0=dt_v[:, :], scalar=0.0, in1=dt_e[:, :],
                                           op0=ALU.max, op1=ALU.add).then_inc(dt_vec_done, 1)
            dve.wait_ge(dt_vec_done, 3)
            nc.vector.tensor_scalar(dt_v[:, :], dt_dt[:, :], dt_par[:, 1:2], -1.0, ALU.mult, ALU.mult).then_inc(dt_vec_done, 1)
            dve.wait_ge(dt_vec_done, 4)
            for c in range(NC):
                cc = slice(c * CH, (c + 1) * CH)
                nc.vector.tensor_tensor_scan(dt_a[:, cc], dt_one[:, :], dt_v[:, cc], 0.0, ALU.mult, ALU.add)\
                  .then_inc(dt_vec_done, 1)
            nc.vector.tensor_copy(dt_small[:, 0:NS], dt_dt[:, TP:T]).then_inc(dt_vec_done, 1)
            dve.wait_ge(dt_tr_done, 1)
            nc.vector.tensor_copy(tokS[:, :, :, :].rearrange("p a c h -> p (a c h)"), ps[:, 4, 0:3 * NC * HEADS])\
              .then_inc(dt_tok_done, 1)
            dve.wait_ge(dt_tok_done, 1)

            def evac_unit(g, t):
                if g is None:
                    return
                pair, half = Pair(group_pair(g) + t // 2), t % 2
                if t >= 4:
                    evac_scaled(pair, half, zs[:, g % 2, t - 4, :])
                    return
                k = 4 * g + t
                slot = 1 - half
                dve.wait_ge(unit_done, pair.unit(half, 1))
                if due(k - 1):
                    dve.wait_ge(tap0_done, k - 1)
                if due(k - 1):
                    dve.wait_ge(cst_tr, k - 1)
                if due(3 * (k - 1)):
                    dve.wait_ge(tap_done, 3 * (k - 1))
                nc.vector.tensor_tensor(raw[:, t % 2, S0 + TAPS - 1:RAW:TAPS], ps[:, 2 * slot + 1, 256:256 + NS],
                                        rstd[:, TP:T], ALU.mult).then_inc(new_evac, 1)
                nc.vector.tensor_tensor(halves(raw[:, t % 2, TAPS - 1:TAPS - 1 + TP]), ps[:, 2 * slot:2 * slot + 2, 0:256],
                                        halves(rstd[:, 0:TP]), ALU.mult).then_inc(evac_done, 1)

            def conv(g, t):
                if g is None:
                    return
                k = 4 * g + t
                dve.wait_ge(tap0_done, k + 1)
                dve.wait_ge(new_evac, k + 1)
                dve.wait_ge(evac_done, Pair(group_pair(g) + t // 2).unit(t % 2, 1))
                for tap in range(1, TAPS):
                    if due(3 * k + tap - 1):
                        dve.wait_ge(tap_done, 3 * k + tap - 1)
                    nc.vector.scalar_tensor_tensor(out=act[:, g % 2, t, :], in0=raw[:, t % 2, tap:tap + CONV_N],
                                                   scalar=convf[:, k, tap:tap + 1], in1=act[:, g % 2, t, :],
                                                   op0=ALU.mult, op1=ALU.add).then_inc(tap_done, 1)

            def low_w(g, i):
                if g is not None:
                    split_w(Pair(group_pair(g) + i))

            def y_norm(g):
                if g < 0:
                    return
                dve.wait_ge(yroot_done, g + 1)
                nc.vector.reciprocal(ssum[:, :], ssum[:, :]).then_inc(yr_done, 1)
                dve.wait_ge(yr_done, g + 1)
                for i in range(2):
                    nc.vector.scalar_tensor_tensor(out=work[:, i, :], in0=work[:, i, :],
                                                   scalar=feat[:, G_SSD + 2 * g + i:G_SSD + 2 * g + i + 1],
                                                   in1=ssum[:, :], op0=ALU.mult, op1=ALU.mult).then_inc(ynorm_done, 1)

            def y_low(g):
                if g < 0:
                    return
                for i in range(2):
                    dve.wait_ge(y_hi_done, 2 * g + i + 1)
                    dve.wait_ge(ynorm_done, 2 * g + i + 1)
                    k = (2 * g + i) % 8
                    nc.vector.tensor_tensor(a_lo[:, k, :], work[:, i, :], a_hi[:, k, :].bitcast(F32), ALU.subtract)\
                      .then_inc(y_lo_done, 1)

            def seg(g, i):
                dve.wait_ge(abc_landed, 16 * (2 * g + i + 1))
                for hh in range(2):
                    h = 4 * g + 2 * i + hh
                    for c in range(NC):
                        ins = nc.vector.tensor_scalar(abc[:, hh, c * CH:(c + 1) * CH], abc[:, hh, c * CH:(c + 1) * CH],
                                                      tokS[:, 2, c, h:h + 1], 0.0, ALU.subtract, ALU.min)
                    ins.then_inc(seg_done, 1)

            def decayed(g, i):
                for hh in range(2):
                    dve.wait_ge(exp_done, 4 * g + 2 * i + hh + 1)
                    dve.wait_ge(cbm_done, g + 1)
                    nc.vector.tensor_tensor(abc[:, hh, :], abc[:, hh, :], cbm[:, :, :].rearrange("p c q -> p (c q)"), ALU.mult)\
                      .then_inc(m_done, 1)

            def sample(g, n):
                k, i, hb = 4 * g + n, n % 2, n // 2
                prod = sq[:, 1, 0:4 * N].rearrange("p (b n) -> p b n", b=4)
                dve.wait_ge(snew_done, k + 1)
                if due(k):
                    dve.wait_ge(sred_done, k)
                if k == 0:
                    dve.wait_ge(ssum_added, 7)
                nc.vector.tensor_tensor(prod, hst[:, :, :], bcs[:, :, N:2 * N], ALU.mult).then_inc(smul_done, 1)
                dve.wait_ge(smul_done, k + 1)
                nc.vector.tensor_reduce(ysmp[:, i, 4 * hb:4 * hb + 4], prod, AX.X, ALU.add).then_inc(sred_done, 1)

            def y_diag(g, i):
                dve.wait_ge(ydiag_done, 2 * g + i + 1)
                if due(2 * g):
                    dve.wait_ge(y_hi_done, 2 * g)
                if due(2 * g):
                    dve.wait_ge(y_lo_done, 2 * g)
                nc.vector.scalar_tensor_tensor(out=work[:, i, 0:TP], in0=act[:, g % 2, 2 + i, 0:TP],
                                               scalar=dtf[:, 2 * g + i, 16:17], in1=ps[:, 4 + i, :],
                                               op0=ALU.mult, op1=ALU.add).then_inc(y1_done, 1)

            def by_head(ap):
                return ap.rearrange("p (h d) -> p h d", d=HD)

            def states(g):
                if due(2 * g):
                    dve.wait_ge(yoff_done, 2 * g)
                if due(g):
                    dve.wait_ge(h4_tr, g)
                for c in range(NC):
                    bank = ps[:, 6 if c < 2 else 4, (c % 2) * 256:(c % 2) * 256 + 256]
                    dve.wait_ge(st_done, 4 * g + (2 if c < 2 else 4))
                    if c == 0:
                        nc.vector.tensor_copy(hprev[:, 0, :], bank).then_inc(hstep_done, 1)
                        continue
                    dve.wait_ge(hstep_done, 4 * g + c)
                    nc.vector.tensor_tensor(by_head(hprev[:, c, :]), by_head(hprev[:, c - 1, :]),
                                            cdec[:, 4 * g:4 * g + 4, c].unsqueeze(2).broadcast_to([P, 4, HD]), ALU.mult)\
                      .then_inc(hchain, 1)
                    dve.wait_ge(hchain, 3 * g + c)
                    nc.vector.tensor_tensor(hprev[:, c, :], hprev[:, c, :], bank, ALU.add).then_inc(hstep_done, 1)

            def combine(g):
                for i in range(2):
                    n = 3 * (2 * g + i)
                    dve.wait_ge(yoff_done, 2 * g + i + 1)
                    dve.wait_ge(ef_done, 2 * g + i + 1)
                    nc.vector.tensor_tensor(abc[:, i, CH:TP], ps[:, 5 + i, CH:TP], abc[:, i, CH:TP], ALU.mult)\
                      .then_inc(cchain, 1)
                    if i == 0:
                        dve.wait_ge(sred_done, 4 * g + 4)
                    nc.vector.scalar_tensor_tensor(out=work[:, i, TP:T], in0=act[:, g % 2, 2 + i, S0:CONV_N:TAPS],
                                                   scalar=dtf[:, 2 * g + i, 16:17], in1=ysmp[:, i, :],
                                                   op0=ALU.mult, op1=ALU.add).then_inc(cchain, 1)
                    dve.wait_ge(cchain, n + 1)
                    dve.wait_ge(y1_done, 2 * g + i + 1)
                    nc.vector.tensor_tensor(work[:, i, CH:TP], work[:, i, CH:TP], abc[:, i, CH:TP], ALU.add)\
                      .then_inc(cchain, 1)
                    dve.wait_ge(cchain, n + 3)
                    dve.wait_ge(z_silu_done, 2 * g + i + 1)
                    nc.vector.tensor_tensor(work[:, i, :], work[:, i, :], zs[:, g % 2, i, :], ALU.mult)\
                      .then_inc(comb_done, 1)

            def window(g, nxt):
                low_w(nxt, 1)
                evac_unit(nxt, 0)
                for i in range(2):
                    dve.wait_ge(xtr_done, 2 * g + i + 1)
                    if due(4 * g):
                        dve.wait_ge(st_done, 4 * g)
                    nc.vector.tensor_tensor(
                        xdt[:, :, i * P:(i + 1) * P].rearrange("p c (h d) -> p c h d", d=HD),
                        ps[:, 4 + i, :].rearrange("p (c h d) -> p c h d", c=NC, d=HD),
                        tokS[:, 0, :, 4 * g + 2 * i:4 * g + 2 * i + 2].unsqueeze(3).broadcast_to([P, NC, 2, HD]),
                        ALU.mult).then_inc(xdt_done, 1)
                y_norm(g - 1)
                seg(g, 0)
                conv(nxt, 0)
                y_low(g - 1)
                evac_unit(nxt, 1)
                dve.wait_ge(cb_done, g + 1)
                if due(4 * g):
                    dve.wait_ge(m_done, 4 * g)
                nc.vector.tensor_tensor(cbm[:, :, :], ps[:, 4, :].rearrange("p (c q) -> p c q", c=NC),
                                        causal[:, :].unsqueeze(1).broadcast_to([P, NC, CH]), ALU.mult)\
                  .then_inc(cbm_done, 1)
                if due(4 * g):
                    dve.wait_ge(outer_done, 4 * g)
                dve.wait_ge(silu_done, 4 * g + 4)
                dve.wait_ge(dtf_landed, 32)
                nc.vector.tensor_tensor(xdts[:, :, :], act[:, g % 2, 2:4, S0:CONV_N:TAPS],
                                        dtf[:, 2 * g:2 * g + 2, 0:NS], ALU.mult).then_inc(xdts_done, 1)
                decayed(g, 0)
                conv(nxt, 1)
                low_w(nxt, 2)
                evac_unit(nxt, 2)
                conv(nxt, 2)
                seg(g, 1)
                decayed(g, 1)
                evac_unit(nxt, 3)
                y_diag(g, 0)
                conv(nxt, 3)
                sample(g, 0)
                low_w(nxt, 3)
                dve.wait_ge(ydiag_done, 2 * g + 2)
                nc.vector.tensor_tensor(xdt[:, :, :].rearrange("p c (h d) -> p c h d", d=HD),
                                        xdt[:, :, :].rearrange("p c (h d) -> p c h d", d=HD),
                                        tokS[:, 1, :, 4 * g:4 * g + 4].unsqueeze(3).broadcast_to([P, NC, 4, HD]),
                                        ALU.mult).then_inc(xdte_done, 1)
                y_diag(g, 1)
                evac_unit(nxt, 4)
                if g == 0:
                    dve.wait_ge(cdec_landed, 16)
                states(g)
                sample(g, 1)
                evac_unit(nxt, 5)
                sample(g, 2)
                sample(g, 3)
                combine(g)

            evac_unit(0, 0)
            conv(0, 0)
            split_w(Pair(2))
            evac_unit(0, 1)
            conv(0, 1)
            evac_unit(0, 2)
            conv(0, 2)
            split_w(Pair(3))
            evac_unit(0, 3)
            conv(0, 3)
            evac_unit(0, 4)
            split_w(Pair(4))
            evac_unit(0, 5)
            for g in range(5):
                window(g, g + 1)

            def out_product(J, n=None, gain=None):
                for i in range(4):
                    split_w(Pair(J + i + 1))
                    for half in range(2):
                        m = 2 * i + half
                        evac_added(Pair(J + i), half, m)
                        if n is not None and m:
                            h_low(n, m - 1, gain)
                if n is not None:
                    h_low(n, KT - 1, gain)

            out_product(J_OUT0)
            window(5, 6)
            window(6, 7)
            window(7, None)
            y_norm(7)
            y_low(7)
            out_product(J_OUT1, 1, G_MLP)

            def a_low(j, count, src):
                dve.wait_ge(a_hi_done, count)
                nc.vector.tensor_tensor(a_lo[:, j % 8, :], src, a_hi[:, j % 8, :].bitcast(F32), ALU.subtract)\
                  .then_inc(a_lo_done, 1)

            def mlp(n, J, last):
                base = 0 if n == 1 else 48

                def chunk(c, first, final):
                    for i in range(4):
                        split_w(Pair(J + i + 1, c * 4))
                        if first and i == 0:
                            inv_rms(n)
                        for half in range(2):
                            j = 2 * i + half
                            U = Pair(J + i, c * 4)
                            t = work[:, half, :]
                            if due(c * 8 + (base + j - 1)):
                                dve.wait_ge(a_lo_done, c * 8 + (base + j - 1))
                            if due(c * 8 + (base + j - 1)):
                                dve.wait_ge(a_hi_done, c * 8 + (base + j - 1))
                            evac_scaled(U, half, t)
                            if j:
                                a_low(j - 1, c * 8 + (base + j), work[:, 1 - half, :])
                            dve.wait_ge(evac_done, U.unit(half, 1))
                            nc.vector.scalar_tensor_tensor(out=t, in0=t, scalar=0.0, in1=t, op0=ALU.max, op1=ALU.mult)\
                              .then_inc(a32_done, 1)
                    a_low(7, c * 8 + (base + 8), work[:, 1, :])
                    for i in range(4):
                        if not (final and last and i == 3):
                            split_w(Pair(J + 4 + i + 1, c * 4))
                        for half in range(2):
                            m = 2 * i + half
                            U = Pair(J + 4 + i, c * 4)
                            evac_added(U, half, m)
                            if final and not last and m:
                                h_low(n + 1, m - 1, G_MIX + KT)
                            if final and last:
                                dve.wait_ge(evac_done, U.unit(half, 1))
                                if due(2 * (m - 1)):
                                    dve.wait_ge(ty_done, 2 * (m - 1))
                                nc.vector.tensor_scalar(xg[:, m % 2, :], xT[:, m, :], feat[:, G_FIN + m:G_FIN + m + 1],
                                                        None, ALU.mult).then_inc(xg_done, 1)
                                if m > 1:
                                    y_rows(m - 2)
                    if final and not last:
                        h_low(n + 1, KT - 1, G_MIX + KT)

                chunk(0, True, False)
                with dve.Fori(1, CHUNKS - 1) as c:
                    chunk(c, False, False)
                chunk(CHUNKS - 1, False, True)

            def y_rows(m):
                dve.wait_ge(ty_done, 2 * m + 2)
                nc.vector.tensor_copy(ytok[:, :, m * P:(m + 1) * P], ps[:, 4 + m % 2, :].rearrange("p (c f) -> p c f", c=NC))\
                  .then_inc(ty_evac, 1)

            mlp(1, J_MLP0, False)

            for i in range(8):
                split_w(Pair(J_V + i + 1))
                if i == 0:
                    inv_rms(2)
                for half in range(2):
                    j = 2 * i + half
                    if due(j - 1):
                        dve.wait_ge(gelu_done, j - 1)
                    evac_scaled(Pair(J_V + i), half, work[:, j % 2, :])
                    if j == 2:
                        dve.wait_ge(mixT_done, 1)
                        for n in range(2):
                            nc.vector.tensor_tensor(wmixT[:, 4 * n:4 * n + 4, :],
                                                    ps[:, 6 + n, :].rearrange("p (g t) -> p g t", t=P),
                                                    causal[:, :].unsqueeze(1).broadcast_to([P, 4, CH]), ALU.mult)\
                              .then_inc(wmask_done, 1)
                    if j:
                        dve.wait_ge(v_tr, j)
                        nc.vector.tensor_copy(vtok[:, :, (j - 1) * P:j * P],
                                              ps[:, 4 + (j - 1) % 2, :].rearrange("p (c f) -> p c f", c=NC))\
                          .then_inc(vtok_done, 1)
            dve.wait_ge(v_tr, 16)
            nc.vector.tensor_copy(vtok[:, :, 15 * P:16 * P], ps[:, 5, :].rearrange("p (c f) -> p c f", c=NC))\
              .then_inc(vtok_done, 1)

            def v_scale():
                dve.wait_ge(vroot_done, 2)
                nc.vector.reciprocal(r_tok[:, :], r_tok[:, :]).then_inc(vrec_done, 1)
                nc.vector.reciprocal(r_smp[:, :], r_smp[:, :]).then_inc(vrec_done, 1)
                dve.wait_ge(vrec_done, 2)
                dve.wait_ge(vtok_done, 16)
                for c in range(NC):
                    nc.vector.tensor_scalar(vtok[:, c, :], vtok[:, c, :], r_tok[:, c:c + 1], None, ALU.mult)\
                      .then_inc(vscaled, 1)

            def v_samples():
                dve.wait_ge(vsmp_done, 16)
                dve.wait_ge(b_landed, 32)
                nc.vector.tensor_tensor(vsmp[:, :, :], vsmp[:, :, :], r_smp[:, :].unsqueeze(1).broadcast_to([P, 16, NS]),
                                        ALU.mult).then_inc(vsn_done, 1)
                dve.wait_ge(vsn_done, 1)
                nc.vector.tensor_tensor(vsmp[:, :, :], vsmp[:, :, :],
                                        feat[:, G_V:G_V + 16].unsqueeze(2).broadcast_to([P, 16, NS]), ALU.mult)\
                  .then_inc(vsn_done, 1)
                dve.wait_ge(vsn_done, 2)
                by_group = "p (g i) b -> p g (i b)"
                nc.vector.tensor_tensor(ssmp.rearrange(by_group, i=2), vsmp.rearrange(by_group, i=2),
                                        w00[:, :, 0].unsqueeze(2).broadcast_to([P, 8, 2 * NS]), ALU.mult)\
                  .then_inc(ssmp_done, 1)
                dve.wait_ge(ssmp_done, 1)
                nc.vector.tensor_tensor(ssmp.rearrange(by_group, i=2), ssmp.rearrange(by_group, i=2),
                                        bmix[:, :, 0].unsqueeze(2).broadcast_to([P, 8, 2 * NS]), ALU.add)\
                  .then_inc(ssmp_done, 1)
                dve.wait_ge(ssmp_done, 2)

            def u_half(first, J):
                for i in range(4):
                    split_w(Pair(J + i + 1))
                    for half in range(2):
                        j = first + 2 * i + half
                        u, s = work[:, j % 2, :], sq[:, j % 2, :]
                        dve.wait_ge(a32_done, 32 + j - 1)
                        evac_scaled(Pair(J + i), half, u)
                        if j == 0:
                            v_scale()
                            v_samples()
                        if j > first:
                            a_low(j - 1, 32 + j, sq[:, 1 - j % 2, :])
                        dve.wait_ge(mixed, j + 1)
                        dve.wait_ge(a_hi_done, 32 + j - 1)
                        dve.wait_ge(a_lo_done, 32 + j - 1)
                        dve.wait_ge(vsum_done, 15)
                        nc.vector.scalar_tensor_tensor(
                            out=s[:, 0:TP].rearrange("p (c t) -> p c t", c=NC),
                            in0=ps[:, 4 + j % 2, :].rearrange("p (c t) -> p c t", c=NC),
                            scalar=feat[:, G_V + j:G_V + j + 1],
                            in1=bmix[:, j // 2, :].unsqueeze(1).broadcast_to([P, NC, CH]),
                            op0=ALU.mult, op1=ALU.add).then_inc(s_done, 1)
                        dve.wait_ge(s_done, j + 1)
                        dve.wait_ge(gelu_done, 16 + j + 1)
                        nc.vector.tensor_tensor(s[:, TP:T], ssmp[:, j, :], u[:, TP:T], ALU.mult).then_inc(gate_done, 1)
                        nc.vector.tensor_tensor(s[:, 0:TP], s[:, 0:TP], u[:, 0:TP], ALU.mult).then_inc(a32_done, 1)
                        if j in (2, 3, 4, 5):
                            n = j - 2
                            dve.wait_ge(vs_tr, n + 1)
                            if due(16 * n):
                                dve.wait_ge(vs_out, 16 * n)
                            nc.vector.tensor_copy(vs_row[:, :, :].rearrange("p a b -> p (a b)"), ps[0:NS, 6 + n % 2, :])\
                              .then_inc(vs_evac, 1)
                dve.wait_ge(a32_done, 32 + first + 8)
                dve.wait_ge(gate_done, first + 8)
                a_low(first + 7, 32 + first + 8, sq[:, 1, :])

            u_half(0, J_U0)
            out_product(J_CMO0)
            u_half(8, J_U1)
            out_product(J_CMO1, 3, G_MLP + KT)
            dve.wait_ge(vs_out, 64)
            mlp(3, J_MLP1, True)
            y_rows(6)
            y_rows(7)
            nc.vector.tensor_copy(ys_row[:, :].rearrange("p (a f) -> p a f", a=2), ps[0:NS, 6:8, :]).then_inc(ty_evac, 1)
            dve.wait_ge(fin_root, 2)
            nc.vector.reciprocal(r_fin[:, 0:NC], r_fin[:, 0:NC]).then_inc(fin_rec, 1)
            nc.vector.reciprocal(r_fin[0:NS, NC:NC + 1], r_fin[0:NS, NC:NC + 1]).then_inc(fin_rec, 1)
            dve.wait_ge(fin_rec, 2)
            dve.wait_ge(ty_evac, 9)
            for c in range(NC):
                nc.vector.tensor_scalar(ytok[:, c, :], ytok[:, c, :], r_fin[:, c:c + 1], None, ALU.mult)\
                  .then_inc(y_scaled, 1)
            nc.vector.tensor_scalar(ys_row[:, :], ys_row[:, :], r_fin[0:NS, NC:NC + 1], None, ALU.mult)\
              .then_inc(y_scaled, 1)


_INS = ("x_prompt x_sample state_ssm state_conv norm_mix_g norm_mlp_g norm_final_g ssd_w_in ssd_conv_w "
        "ssd_conv_b ssd_dt_bias ssd_a_log ssd_d ssd_norm_g ssd_w_out cm_w_in cm_b_in cm_v_norm_g cm_w_s "
        "cm_b_s cm_w_out mlp_w_up mlp_w_down").split()
_OUTS = ((1, TP, D), (NS, 1, D), (1, 1, HEADS, HD, N), (1, 1, TAPS - 1, CONVD), (1, NS, HEADS, HD, N),
         (1, NS, TAPS - 1, CONVD), (1, NS, 1, CMW))


def kernel(**inputs):
    import numpy as np
    import concourse.bacc as bacc
    from concourse.bass_utils import run_bass_kernel_spmd

    nc = bacc.Bacc("TRN2", target_bir_lowering=False, num_devices=1)
    arrays, args = {}, []
    for name in _INS:
        a = np.ascontiguousarray(inputs[name])
        arrays["in_" + name] = a
        args.append(nc.dram_tensor("in_" + name, a.shape, mybir.dt.from_np(a.dtype), kind="ExternalInput").ap())
    for i, shape in enumerate(_OUTS):
        args.append(nc.dram_tensor(f"out_{i}", shape, F32, kind="ExternalOutput").ap())
    hybrid_step(nc, *args)
    r = run_bass_kernel_spmd(nc, [arrays], core_ids=[0])
    return tuple(r.results[0][f"out_{i}"] for i in range(len(_OUTS)))
```

```python
from contextlib import ExitStack

import concourse.bass as bass
from concourse import mybir

F32 = mybir.dt.float32
F32R = mybir.dt.float32r
ACT = mybir.ActivationFunctionType
ALU = mybir.AluOpType
AX = mybir.AxisListType

P = 128
D = 1024
KT = D // P
TP = 512
NS = 8
T = TP + NS
TH = T // 2
CH = 128
NC = TP // CH
DI = 2048
HEADS = 32
GROUPS = 8
HD = 64
N = 128
CONVD = DI + 2 * GROUPS * N
TAPS = 4
CMW = 2048
FF = 4096
EPS = 1e-5
RAW = TAPS - 1 + TP + NS * TAPS
CONV_N = RAW - TAPS + 1
S0 = TP + TAPS - 1
CHUNKS = FF // D

EVEN = ((0, TH), (TH, TH))
PROMPT = ((0, 256), (256, T - 256))


class Pair:

    def __init__(self, s, loop=0):
        self.s, self.loop = s, loop
        self.slot = s % 2

    def times(self, k, c):
        return self.loop * (2 * k) + (k * self.s + c)

    def unit(self, half, c=0):
        if self.s > J_TAIL:
            c += KT - 2
        return self.times(2, c) if half else self.times(2, c - 1)

    def multiplied(self):
        return self.times(2, 1 + (KT - 2 if self.s >= J_TAIL else 0))

    def tiles(self):
        return KT - 2 if J_OUT1 <= self.s < J_TAIL else KT

    def use(self, c=0):
        return self.loop + (self.s // 2 + c)


J_DT = 0
J_OUT0 = 1 + 3 * 5 + 2
J_OUT1 = 1 + 3 * GROUPS + 4
J_TAIL = J_OUT1 + 4
J_MLP0 = J_TAIL + 1
J_V = J_MLP0 + 8 * CHUNKS
J_U0 = J_V + 8
J_CMO0 = J_U0 + 4
J_U1 = J_CMO0 + 4
J_CMO1 = J_U1 + 4
J_MLP1 = J_CMO1 + 4
J_END = J_MLP1 + 8 * CHUNKS


def group_pair(g, k):
    s = 1 + 3 * g + k
    return s + 4 if s >= J_OUT0 else s


def c_columns(pair):
    groups = {group_pair(g, 0): g for g in range(GROUPS)}
    return 16 * (groups[pair.s] + 1) if pair.s in groups and isinstance(pair.loop, int) else 0


def hybrid_step(nc, x_prompt, x_sample, state_ssm, state_conv, norm_mix_g, norm_mlp_g,
                norm_final_g, ssd_w_in, ssd_conv_w, ssd_conv_b, ssd_dt_bias, ssd_a_log, ssd_d,
                ssd_norm_g, ssd_w_out, cm_w_in, cm_b_in, cm_v_norm_g, cm_w_s, cm_b_s, cm_w_out,
                mlp_w_up, mlp_w_down, y_prompt, y_sample, ssm_prompt, conv_prompt, ssm_sample,
                conv_sample, cm_v_sample):
    ctx = ExitStack()
    with ctx:
        def sb(name, shape, dt=F32):
            return ctx.enter_context(nc.sbuf_tensor(name, shape, dt))

        def sem(name):
            return ctx.enter_context(nc.semaphore(name))

        xT = sb("xT", [P, KT, T])
        h_hi = sb("h_hi", [P, KT, T], F32R)
        h_lo = sb("h_lo", [P, KT, T], F32R)
        a_hi = sb("a_hi", [P, KT, T], F32R)
        a_lo = sb("a_lo", [P, KT, T], F32R)
        w32 = sb("w32", [P, 2, KT, 256])
        w_hi = sb("w_hi", [P, 2, KT, 256], F32R)
        w_lo = sb("w_lo", [P, 2, KT, 256], F32R)
        rstd = sb("rstd", [P, T])
        ssum = sb("ssum", [P, T])
        sq = sb("sq", [P, 2, T])
        work = sb("work", [P, 2, T])
        ident = sb("ident", [P, P])
        causal = sb("causal", [P, P])
        ones = sb("ones", [P, 1])
        eps = sb("eps", [P, 1])
        FEAT = 40 + 16 + 32 + 16
        feat = sb("feat", [P, FEAT])
        CW = 5 + 3 * NS
        convf = sb("convf", [P, 32, CW])
        tokS = sb("tokS", [P, 3, NC, HEADS])
        dtf = sb("dtf", [P, 16, 20])
        cdec = sb("cdec", [P, HEADS, NC])
        ARENA = 14728
        arena = sb("arena", [P, ARENA])

        G_MIX, G_MLP, G_FIN, G_SSD, B_CM, G_V = 0, 16, 32, 40, 56, 88

        at = [0]

        def carve(*shape, parts=P):
            n = 1
            for d in shape:
                n *= d
            ap = arena[0:parts, at[0]:at[0] + n]
            at[0] += n
            assert at[0] <= ARENA, at[0]
            if len(shape) == 2:
                return ap.rearrange("p (a b) -> p a b", a=shape[0])
            if len(shape) == 3:
                return ap.rearrange("p (a b c) -> p a b c", a=shape[0], b=shape[1])
            return ap

        act = carve(2, 4, CONV_N)
        raw = carve(2, RAW + 1)
        dt_at = at[0]
        zs = carve(2, T)
        abc = carve(2, 2, TP)
        xdt = carve(NC, 4 * HD)
        Btok = carve(NC, N)
        cbm = carve(NC, CH)
        hprev = carve(NC, 4 * HD)
        hst = carve(2, 4, N)
        outer = carve(2, N)
        bcs = carve(2, 2, 2 * N)
        cstage = carve(4, P, parts=35)
        bcrow = arena[64:72, at[0] - 512:at[0] - 256]
        ssm_stage = carve(2, N)
        xdts = carve(2, NS)
        ysmp = carve(2, NS)
        at[0] = dt_at
        dt_v = carve(T, parts=HEADS)
        dt_e = carve(T, parts=HEADS)
        dt_dt = carve(T, parts=HEADS)
        dt_a = carve(T, parts=HEADS)
        dt_end = carve(NC, CH, parts=HEADS)
        dt_small = carve(24, parts=HEADS)
        dt_par = carve(4, parts=HEADS)
        dt_one = carve(CH, parts=HEADS)
        at[0] = 0
        xtok = carve(NC, D)
        xs_row = carve(D, parts=NS)
        crow = carve(32, P, parts=CW)
        frow = carve(P, parts=FEAT)
        at[0] = 0
        vtok = carve(NC, CMW)
        wmix = carve(8, CH)
        wmixT = carve(8, CH)
        bmix = carve(8, CH)
        gv = carve(2, T)
        vsmp = carve(16, NS)
        ssmp = carve(16, NS)
        w00 = carve(8, 2)
        r_tok = carve(4)
        r_smp = carve(NS)
        vs_row = carve(4, P, parts=NS)
        at[0] = 0
        ytok = carve(NC, D)
        ys_row = carve(D, parts=NS)
        xg = carve(2, T)
        r_fin = carve(8)

        ps = ctx.enter_context(nc.psum_tensor("ps", [P, 8, 512], F32))

        def psum_tok(slot):
            return ps[:, 2 * slot:2 * slot + 2, 0:TH]

        def halves(ap):
            return ap.rearrange("p (a b) -> p a b", a=2)

        scr_a = nc.dram_tensor("scr_a", (HEADS, TP), F32, kind="Internal").ap()
        scr_s = nc.dram_tensor("scr_s", (HEADS, 24), F32, kind="Internal").ap()
        scr_bc = nc.dram_tensor("scr_bc", (GROUPS, NS, 2 * N), F32, kind="Internal").ap()

        def by_rows(w):
            return w[:, J_TAIL % 2].rearrange("p (a k) n -> p a (k n)", a=2)

        w_landed = [sem("w_landed0"), sem("w_landed1")]
        c_landed = sem("c_landed")
        w_hi_done = sem("w_hi_done")
        w_lo_done = sem("w_lo_done")
        unit_done = sem("unit_done")
        evac_done = sem("evac_done")
        h_hi_ready = sem("h_hi_ready")
        h_lo_ready = sem("h_lo_ready")
        sq_ready = sem("sq_ready")
        ssum_added = sem("ssum_added")
        stats_done = sem("stats_done")
        root_done = sem("root_done")
        r_ready = sem("r_ready")
        x_landed = sem("x_landed")
        xs_landed = sem("xs_landed")
        crow_landed = sem("crow_landed")
        frow_landed = sem("frow_landed")
        par_landed = sem("par_landed")
        ident_ready = sem("ident_ready")
        const_ready = sem("const_ready")
        w_cleared = sem("w_cleared")
        xt_done = sem("xt_done")
        crow_done = sem("crow_done")
        frow_done = sem("frow_done")
        x_ready = sem("x_ready")
        xs_ready = sem("xs_ready")
        convf_ready = sem("convf_ready")
        feat_ready = sem("feat_ready")
        raw_zeroed = sem("raw_zeroed")
        dt_act_done = sem("dt_act_done")
        dt_vec_done = sem("dt_vec_done")
        dt_tr_done = sem("dt_tr_done")
        dt_tok_done = sem("dt_tok_done")
        scr_a_done = sem("scr_a_done")
        scr_s_done = sem("scr_s_done")
        dtf_landed = sem("dtf_landed")
        cdec_landed = sem("cdec_landed")
        sraw_filled = sem("sraw_filled")
        new_evac = sem("new_evac")
        tap0_done = sem("tap0_done")
        tap_done = sem("tap_done")
        silu_done = sem("silu_done")
        z_silu_done = sem("z_silu_done")
        cst_tr = sem("cst_tr")
        cst_evac = sem("cst_evac")
        cst_out = sem("cst_out")
        xtr_done = sem("xtr_done")
        xdt_done = sem("xdt_done")
        Btr_done = sem("Btr_done")
        Btok_done = sem("Btok_done")
        cb_done = sem("cb_done")
        cbm_done = sem("cbm_done")
        bc_tr = sem("bc_tr")
        bc_evac = sem("bc_evac")
        bc_out = sem("bc_out")
        bcs_landed = [sem("bcs_landed0"), sem("bcs_landed1")]
        xdts_done = sem("xdts_done")
        hst_landed = [sem("hst_landed0"), sem("hst_landed1")]
        decay_done = sem("decay_done")
        outer_done = sem("outer_done")
        state_added = sem("state_added")
        sstored = [sem("sstored0"), sem("sstored1")]
        smul_done = sem("smul_done")
        sred_done = sem("sred_done")
        abc_landed = [sem("abc_landed0"), sem("abc_landed1")]
        seg_done = sem("seg_done")
        exp_done = sem("exp_done")
        m_done = sem("m_done")
        ydiag_done = sem("ydiag_done")
        y1_done = sem("y1_done")
        xdte_done = sem("xdte_done")
        st_done = sem("st_done")
        hstep_done = sem("hstep_done")
        yoff_done = sem("yoff_done")
        ef_landed = sem("ef_landed")
        ef_done = sem("ef_done")
        comb_done = sem("comb_done")
        ysq_done = sem("ysq_done")
        ysum_done = sem("ysum_done")
        rms_done = sem("rms_done")
        yroot_done = sem("yroot_done")
        yr_done = sem("yr_done")
        ynorm_done = sem("ynorm_done")
        y_hi_done = sem("y_hi_done")
        y_lo_done = sem("y_lo_done")
        h4_tr = sem("h4_tr")
        h4_evac = sem("h4_evac")
        ssm_out = sem("ssm_out")
        last_ssm_out = sem("last_ssm_out")
        conv_old = sem("conv_old")
        a_hi_done = sem("a_hi_done")
        a_lo_done = sem("a_lo_done")
        a32_done = sem("a32_done")
        mix_landed = sem("mix_landed")
        mixT_done = sem("mixT_done")
        wmask_done = sem("wmask_done")
        b_landed = sem("b_landed")
        gelu_done = sem("gelu_done")
        v_tr = sem("v_tr")
        vtok_done = sem("vtok_done")
        vsq_done = sem("vsq_done")
        vsum_done = sem("vsum_done")
        vstat_done = sem("vstat_done")
        vroot_done = sem("vroot_done")
        vrec_done = sem("vrec_done")
        vscaled = sem("vscaled")
        vscaled_act = sem("vscaled_act")
        vsmp_done = sem("vsmp_done")
        ssmp_done = sem("ssmp_done")
        s_done = sem("s_done")
        mixed = sem("mixed")
        gate_done = sem("gate_done")
        vsn_done = sem("vsn_done")
        y_scaled = sem("y_scaled")
        y_scaled_act = sem("y_scaled_act")
        cchain = sem("cchain")
        hchain = sem("hchain")
        vs_tr = sem("vs_tr")
        vs_evac = sem("vs_evac")
        vs_out = sem("vs_out")
        ty_done = sem("ty_done")
        ty_evac = sem("ty_evac")
        fin_stat = sem("fin_stat")
        fin_root = sem("fin_root")
        fin_rec = sem("fin_rec")
        xg_done = sem("xg_done")
        out_done = sem("out_done")

        def due(count):
            return not isinstance(count, int) or count > 0

        block = ctx.enter_context(nc.Block())

        def w_block(dram, row0, col0, n=256):
            return dram[bass.ds(row0, D), bass.ds(col0, n)].rearrange("(k p) n -> p k n", p=P)

        w_in, w_out = ssd_w_in[0], ssd_w_out[0]
        c_in, c_out = cm_w_in[0], cm_w_out[0]

        @block.sync
        def _(sp):
            def stage(pair, src, dst=None):
                if due(pair.times(1, -1)):
                    sp.wait_ge(w_hi_done, pair.times(1, -1))
                    sp.wait_ge(w_lo_done, pair.times(1, -1))
                sp.dma_start(w32[:, pair.slot] if dst is None else dst, src).then_inc(w_landed[pair.slot], 16)

            def group(g, k):
                J = group_pair(g, k)
                if k:
                    stage(Pair(J), w_block(w_in, 0, (DI if k == 1 else 0) + g * 256))
                else:
                    stage(Pair(J), w_block(w_in, 0, 2 * DI + g * N, N), w32[:, J % 2, :, 0:N])
                    sp.dma_start(w32[:, J % 2, :, N:2 * N], w_block(w_in, 0, 2 * DI + (GROUPS + g) * N, N))\
                      .then_inc(c_landed, 16)

            def run(J, dram, row0, col0, n):
                for i in range(n):
                    stage(Pair(J + i), w_block(dram, row0, col0 + 256 * i))

            def mlp(J, layer):
                up, down = mlp_w_up[layer], mlp_w_down[layer]
                with sp.Fori(0, CHUNKS) as c:
                    for i in range(4):
                        stage(Pair(J + i, c * 4), w_block(up, 0, c * D + 256 * i))
                    for i in range(4):
                        stage(Pair(J + 4 + i, c * 4), w_block(down, c * D, 256 * i))

            def store_state(g):
                if g < 0:
                    return
                sp.wait_ge(h4_evac, g + 1)
                for i in range(2):
                    h0 = 4 * g + 2 * i
                    sp.dma_start(ssm_prompt[0, 0, h0:h0 + 2].rearrange("h p n -> (h p) n"), ssm_stage[:, i, :])\
                        .then_inc(ssm_out, 16)

            def store_conv(g):
                sp.wait_ge(cst_evac, g + 1)
                x0, b0 = 2 * g * P, DI + g * N
                for row, dst in ((slice(0, 3), conv_prompt[0, 0]), (slice(6, 35, 4), conv_sample[0, :, 2])):
                    sp.dma_start(dst[:, x0:x0 + 2 * P], cstage[row, 2:4, :]).then_inc(cst_out, 16)
                    sp.dma_start(dst[:, DI:DI + 2 * GROUPS * N].rearrange("r (b c) -> r b c", b=2)[:, :, g * N:(g + 1) * N],
                                   cstage[row, 0:2, :]).then_inc(cst_out, 16)

            for c in range(NC):
                sp.dma_start(xtok[:, c, :], x_prompt[0, c * P:(c + 1) * P, :]).then_inc(x_landed, 16)
            sp.wait_ge(w_cleared, 1)
            sp.dma_start(w32[:, 0, :, 0:HEADS], w_block(w_in, 0, DI + CONVD, HEADS)).then_inc(w_landed[0], 16)
            for g in range(GROUPS):
                group(g, 0)
                group(g, 1)
                if g == 5:
                    run(J_OUT0, w_out, 0, 0, 1)
                else:
                    group(g, 2)
                if g:
                    store_conv(g - 1)
                    store_state(g - 2)
                if g == 5:
                    for i in range(1, 4):
                        stage(Pair(J_OUT0 + i), w_block(w_out, 0, 256 * i))
                    group(g, 2)
            for i in range(4):
                n = 256 * i
                stage(Pair(J_OUT1 + i), w_out[D:DI - 2 * P, n:n + 256].rearrange("(k p) n -> p k n", p=P),
                      w32[:, (J_OUT1 + i) % 2, 0:KT - 2])
                if i == 2:
                    store_conv(7)
                    store_state(6)
            stage(Pair(J_TAIL), w_out[DI - 2 * P:DI, :].rearrange("(k p) n -> p k n", p=P), by_rows(w32))
            mlp(J_MLP0, 0)
            run(J_V, c_in, 0, CMW, 8)
            run(J_U0, c_in, 0, 0, 4)
            run(J_CMO0, c_out, 0, 0, 4)
            run(J_U1, c_in, 0, D, 4)
            run(J_CMO1, c_out, D, 0, 4)
            mlp(J_MLP1, 1)
            for c in range(NC):
                sp.wait_ge(y_scaled_act if c % 2 else y_scaled, c // 2 + 1)
                sp.dma_start(y_prompt[0, c * P:(c + 1) * P, :], ytok[:, c, :]).then_inc(out_done, 16)
            sp.wait_ge(y_scaled, NC // 2 + 1)
            sp.dma_start(y_sample.rearrange("b s d -> (b s) d"), ys_row[:, :]).then_inc(out_done, 16)
            sp.wait_ge(out_done, 80)

        @block.tensor
        def _(pe):
            def unit(pair, half, hi, lo, split=EVEN, k_ready=None):
                only = pair.s == J_DT and isinstance(pair.loop, int)
                if half == 0 or only:
                    pe.wait_ge(w_hi_done, pair.times(1, 1))
                    pe.wait_ge(w_lo_done, pair.times(1, 1))
                if due(pair.unit(half, -1)):
                    pe.wait_ge(evac_done, pair.unit(half, -1))
                slot, col = 1 - half, 0 if only else half * P
                tiles = pair.tiles()
                for k in range(tiles):
                    if k_ready:
                        k_ready(k)
                    for n, (w, x) in enumerate(((w_hi, hi), (w_hi, lo), (w_lo, hi))):
                        for b, (t0, tn) in enumerate(split):
                            mm = pe.matmul(ps[:, 2 * slot + b, 0:tn],
                                           w[:, pair.slot, k, col:col + P],
                                           x[:, k, t0:t0 + tn],
                                           start=(k == 0 and n == 0),
                                           stop=(k == tiles - 1 and n == 2))
                mm.then_inc(unit_done, 1)

            def tail_unit(m):
                if m == 0:
                    pe.wait_ge(w_hi_done, J_TAIL + 1)
                    pe.wait_ge(w_lo_done, J_TAIL + 1)
                pe.wait_ge(evac_done, Pair(J_TAIL).unit(0, m - 1))
                slot = 1 - m % 2
                for k in range(2):
                    if m == 0:
                        pe.wait_ge(y_hi_done, 2 * 7 + k + 1)
                        pe.wait_ge(y_lo_done, 2 * 7 + k + 1)
                    for n, (w, x) in enumerate(((w_hi, a_hi), (w_hi, a_lo), (w_lo, a_hi))):
                        for b, (t0, tn) in enumerate(EVEN):
                            mm = pe.matmul(ps[:, 2 * slot + b, 0:tn], by_rows(w)[:, k, m * P:(m + 1) * P],
                                           x[:, KT - 2 + k, t0:t0 + tn],
                                           start=(k == 0 and n == 0), stop=(k == 1 and n == 2))
                mm.then_inc(unit_done, 1)

            def h_ready(n):
                def ready(k):
                    pe.wait_ge(h_hi_ready, 8 * n + k + 1)
                    pe.wait_ge(h_lo_ready, 8 * n + k + 1)
                return ready

            def stats(n):
                pe.wait_ge(ssum_added, 7 * (n + 1))
                if due(n):
                    pe.wait_ge(root_done, n)
                if n == 1:
                    pe.wait_ge(comb_done, 16)
                    pe.wait_ge(h4_evac, 8)
                if n == 3:
                    pe.wait_ge(s_done, 16)
                for b in range(2):
                    mm = pe.matmul(ps[:, 4 + b, 0:TH], ones[:, 0:1].to_broadcast([P, P]),
                                   ssum[:, b * TH:(b + 1) * TH], start=True, stop=True)
                mm.then_inc(stats_done, 1)

            pe.wait_ge(ident_ready, 4)
            pe.wait_ge(x_landed, 64)
            for m in range(KT):
                if due(m - 1):
                    pe.wait_ge(x_ready, m - 1)
                for c in range(NC):
                    mm = pe.transpose(ps[:, 4 + m % 2, c * P:(c + 1) * P], xtok[:, c, m * P:(m + 1) * P], ident[:, :])
                mm.then_inc(xt_done, 1)
                if m == 0:
                    pe.wait_ge(xs_landed, 16)
                    for k in range(KT):
                        mm = pe.transpose(ps[:, 6, k * NS:(k + 1) * NS], xs_row[:, k * P:(k + 1) * P],
                                          ident[0:NS, 0:NS])
                    pe.wait_ge(frow_landed, 96)
                    pe.transpose(ps[:, 6, 128:128 + FEAT], frow[:, :], ident[0:FEAT, 0:FEAT]).then_inc(frow_done, 1)
            pe.wait_ge(crow_landed, 144)
            pe.wait_ge(feat_ready, 1)
            pe.wait_ge(xs_ready, 1)
            for half in range(2):
                for i in range(16):
                    mm = pe.transpose(ps[:, 6 + half, i * CW:(i + 1) * CW], crow[:, 16 * half + i, :],
                                      ident[0:CW, 0:CW])
                mm.then_inc(crow_done, 1)

            def raw_tr(g, t):
                pe.wait_ge(evac_done, Pair(group_pair(g, t // 2)).unit(t % 2, 1))
                pe.wait_ge(sraw_filled, 4 * g + t + 1)
                if t == 0:
                    if due(g):
                        pe.wait_ge(cst_evac, g)
                    pe.wait_ge(crow_done, 2)
                    pe.wait_ge(convf_ready, 2)
                    if due(g - 1):
                        pe.wait_ge(yroot_done, g - 1)
                pe.transpose(ps[0:35, 7, t * P:(t + 1) * P], raw[:, t % 2, TP:TP + 35], ident[:, :])\
                  .then_inc(cst_tr, 1)

            def y_ready(first):
                def ready(k):
                    pe.wait_ge(y_hi_done, 2 * first + k + 1)
                    pe.wait_ge(y_lo_done, 2 * first + k + 1)
                return ready

            def gu(g, u):
                if g == GROUPS:
                    unit(Pair(J_OUT1 + u // 2), u % 2, a_hi, a_lo, k_ready=y_ready(4) if u == 0 else None)
                else:
                    unit(Pair(group_pair(g, u // 2)), u % 2, h_hi, h_lo, PROMPT if u < 4 else EVEN)

            def rms(g):
                if g < 0:
                    return
                pe.wait_ge(ysum_done, g + 1)
                pe.wait_ge(cst_evac, min(g + 2, GROUPS))
                pe.wait_ge(comb_done, 2 * g + 2)
                for b in range(2):
                    mm = pe.matmul(ps[:, 6 + b, 0:TH], ones[:, 0:1].to_broadcast([P, P]),
                                   ssum[:, b * TH:(b + 1) * TH], start=True, stop=True)
                mm.then_inc(rms_done, 1)

            def state_out(g):
                if g < 0:
                    return
                pe.wait_ge(hstep_done, 4 * g + 4)
                pe.wait_ge(comb_done, 2 * g + 1)
                for i in range(2):
                    mm = pe.transpose(ps[:, 5, 256 + i * N:256 + (i + 1) * N], hprev[:, 3, i * P:(i + 1) * P], ident[:, :])
                mm.then_inc(h4_tr, 1)

            def window(g):
                nxt, A = g + 1, act[:, g % 2]
                gu(g, 4)
                raw_tr(g, 3)
                pe.wait_ge(silu_done, 4 * g + 2)
                pe.wait_ge(dt_tok_done, 1)
                if due(4 * g):
                    pe.wait_ge(hstep_done, 4 * g)
                for c in range(NC):
                    mm = pe.matmul(ps[:, 4, c * CH:(c + 1) * CH], A[:, 0, c * CH:(c + 1) * CH],
                                   A[:, 1, c * CH:(c + 1) * CH], start=True, stop=True)
                mm.then_inc(cb_done, 1)
                if due(2 * g - 1):
                    pe.wait_ge(comb_done, 2 * g - 1)
                state_out(g - 1)
                for i in range(2):
                    mm = pe.transpose(ps[0:NS, 5, i * N:(i + 1) * N], A[:, i, S0:CONV_N:TAPS], ident[:, :])
                mm.then_inc(bc_tr, 1)
                gu(g, 5)
                pe.wait_ge(silu_done, 4 * g + 4)
                for i in range(2):
                    if i == 0:
                        pe.wait_ge(cbm_done, g + 1)
                    else:
                        pe.wait_ge(bc_evac, g + 1)
                        if due(g):
                            pe.wait_ge(h4_evac, g)
                    for c in range(NC):
                        mm = pe.transpose(ps[:, 4 + i, c * P:(c + 1) * P], A[:, 2 + i, c * CH:(c + 1) * CH], ident[:, :])
                    mm.then_inc(xtr_done, 1)
                rms(g - 1)
                if nxt < GROUPS:
                    gu(nxt, 0)
                for i in range(2):
                    pe.wait_ge(xdt_done, 2 * g + i + 1)
                    for hh in range(2):
                        pe.wait_ge(m_done, 4 * g + 2 * i + hh + 1)
                        for c in range(NC):
                            mm = pe.matmul(ps[hh * HD:(hh + 1) * HD, 4 + i, c * CH:(c + 1) * CH],
                                           xdt[:, c, (2 * i + hh) * HD:(2 * i + hh + 1) * HD],
                                           abc[:, i, hh, c * CH:(c + 1) * CH], start=True, stop=True)
                    mm.then_inc(ydiag_done, 1)
                    if i == 0:
                        if due(g):
                            pe.wait_ge(yroot_done, g)
                        for c in range(NC):
                            mm = pe.transpose(ps[:, 6, c * P:(c + 1) * P], A[:, 0, c * CH:(c + 1) * CH], ident[:, :])
                        mm.then_inc(Btr_done, 1)
                        if nxt == GROUPS:
                            gu(nxt, 0)
                        gu(nxt, 1)
                        if nxt < GROUPS:
                            raw_tr(nxt, 0)
                if nxt < GROUPS:
                    raw_tr(nxt, 1)
                gu(nxt, 2)
                pe.wait_ge(xdte_done, g + 1)
                pe.wait_ge(Btok_done, g + 1)
                for c in range(NC):
                    if c == 2:
                        pe.wait_ge(y1_done, 2 * g + 1)
                    mm = pe.matmul(ps[:, 6 if c < 2 else 4, (c % 2) * 256:(c % 2) * 256 + 256],
                                   Btok[:, c, :], xdt[:, c, :], start=True, stop=True)
                    mm.then_inc(st_done, 1)
                gu(nxt, 3)
                if nxt < GROUPS:
                    raw_tr(nxt, 2)
                pe.wait_ge(y1_done, 2 * g + 2)
                for i in range(2):
                    for c in range(1, NC):
                        if i == 0:
                            pe.wait_ge(hstep_done, 4 * g + c)
                        mm = pe.matmul(ps[:, 5 + i, c * CH:(c + 1) * CH], hprev[:, c - 1, i * P:(i + 1) * P],
                                       A[:, 1, c * CH:(c + 1) * CH], start=True, stop=True)
                    mm.then_inc(yoff_done, 1)

            pe.wait_ge(const_ready, 2)
            pe.wait_ge(x_ready, 8)
            unit(Pair(J_DT), 1, h_hi, h_lo, k_ready=h_ready(0))
            stats(0)
            gu(0, 0)
            gu(0, 1)
            gu(0, 2)
            pe.wait_ge(dt_vec_done, 9)
            pe.wait_ge(dt_act_done, 10)
            pe.wait_ge(root_done, 1)
            for n, src in enumerate((dt_dt, dt_end.rearrange("p a b -> p (a b)"), dt_a)):
                for c in range(NC):
                    j = n * NC + c
                    mm = pe.transpose(ps[:, 4, j * HEADS:(j + 1) * HEADS], src[:, c * CH:(c + 1) * CH],
                                      ident[0:HEADS, 0:HEADS])
            mm.then_inc(dt_tr_done, 1)

            raw_tr(0, 0)
            gu(0, 3)
            raw_tr(0, 1)
            raw_tr(0, 2)
            for g in range(5):
                window(g)

            def out_product(J, k_ready):
                for i in range(4):
                    for half in range(2):
                        unit(Pair(J + i), half, a_hi, a_lo, k_ready=k_ready if i == half == 0 else None)

            out_product(J_OUT0, y_ready(0))
            for g in range(5, GROUPS):
                window(g)
            gu(GROUPS, 4)
            gu(GROUPS, 5)
            rms(7)
            state_out(7)
            gu(GROUPS, 6)
            gu(GROUPS, 7)
            for m in range(KT):
                tail_unit(m)

            def out_tr(m):
                pe.wait_ge(xg_done, m + 1)
                if due(m - 1):
                    pe.wait_ge(ty_evac, m - 1)
                if m == 0:
                    pe.wait_ge(root_done, 4)
                for c in range(NC):
                    mm = pe.transpose(ps[:, 4 + m % 2, c * P:(c + 1) * P], xg[:, m % 2, c * CH:(c + 1) * CH], ident[:, :])
                mm.then_inc(ty_done, 1)
                pe.transpose(ps[0:NS, 6 + m // 4, (m % 4) * P:(m % 4 + 1) * P], xg[:, m % 2, TP:T], ident[:, :])\
                  .then_inc(ty_done, 1)

            def mlp(n, J):
                def chunk(c, first, final=False):
                    for i in range(4):
                        for half in range(2):
                            unit(Pair(J + i, c * 4), half, h_hi, h_lo,
                                 k_ready=h_ready(n) if first and i == half == 0 else None)
                            if first and i == half == 0:
                                stats(n)
                    for i in range(4):
                        for half in range(2):
                            done = 0 if n == 1 else 48

                            def ready(k):
                                pe.wait_ge(a_hi_done, c * 8 + (done + k + 1))
                                pe.wait_ge(a_lo_done, c * 8 + (done + k + 1))

                            unit(Pair(J + 4 + i, c * 4), half, a_hi, a_lo,
                                 k_ready=ready if i == half == 0 else None)
                            if final and n == 3 and i + half:
                                out_tr(2 * i + half - 1)
                chunk(0, True)
                with pe.Fori(1, CHUNKS - 1) as c:
                    chunk(c, False)
                chunk(CHUNKS - 1, False, final=True)

            mlp(1, J_MLP0)

            for i in range(8):
                for half in range(2):
                    j = 2 * i + half
                    unit(Pair(J_V + i), half, h_hi, h_lo, k_ready=h_ready(2) if j == 0 else None)
                    if j == 0:
                        stats(2)
                    if j == 1:
                        pe.wait_ge(mix_landed, 16)
                        for g in range(8):
                            mm = pe.transpose(ps[:, 6 + g // 4, (g % 4) * P:(g % 4 + 1) * P], wmix[:, g, :], ident[:, :])
                        mm.then_inc(mixT_done, 1)
                    if j >= 1:
                        tile = j - 1
                        pe.wait_ge(gelu_done, tile + 1)
                        if due(tile - 1):
                            pe.wait_ge(vtok_done, tile - 1)
                        pe.wait_ge(root_done, 3)
                        for c in range(NC):
                            mm = pe.transpose(ps[:, 4 + tile % 2, c * P:(c + 1) * P],
                                              gv[:, tile % 2, c * CH:(c + 1) * CH], ident[:, :])
                        mm.then_inc(v_tr, 1)
            pe.wait_ge(gelu_done, 16)
            pe.wait_ge(vtok_done, 14)
            for c in range(NC):
                mm = pe.transpose(ps[:, 5, c * P:(c + 1) * P], gv[:, 1, c * CH:(c + 1) * CH], ident[:, :])
            mm.then_inc(v_tr, 1)

            def v_stats():
                pe.wait_ge(vsum_done, 15)
                pe.wait_ge(vtok_done, 16)
                for c in range(NC):
                    pe.matmul(ps[:, 4, c:c + 1], ssum[:, c * CH:(c + 1) * CH], ones[:, 0:1], start=True, stop=True)
                pe.matmul(ps[:, 4, 8:8 + NS], ones[:, 0:1].to_broadcast([P, P]), ssum[:, TP:T],
                          start=True, stop=True).then_inc(vstat_done, 1)

            def v_rows(n):
                pe.wait_ge(vsn_done, 2)
                if due(n - 1):
                    pe.wait_ge(vs_evac, n - 1)
                for i in range(4):
                    mm = pe.transpose(ps[0:NS, 6 + n % 2, i * P:(i + 1) * P], vsmp[:, 4 * n + i, :], ident[:, :])
                mm.then_inc(vs_tr, 1)

            def mix(j):
                if due(j - 1):
                    pe.wait_ge(s_done, j - 1)
                for c in range(NC):
                    mm = pe.matmul(ps[:, 4 + j % 2, c * CH:(c + 1) * CH], vtok[:, c, j * P:(j + 1) * P],
                                   wmixT[:, j // 2, :], start=True, stop=True)
                mm.then_inc(mixed, 1)

            def u_half(first, J):
                for i in range(4):
                    for half in range(2):
                        j = first + 2 * i + half
                        unit(Pair(J + i), half, h_hi, h_lo)
                        if j == 0:
                            v_stats()
                            continue
                        if j == 1:
                            pe.wait_ge(wmask_done, 2)
                            pe.wait_ge(vrec_done, 2)
                            pe.wait_ge(vscaled, 2)
                            pe.wait_ge(vscaled_act, 2)
                            mix(0)
                        mix(j)
                        if 1 <= j < 5:
                            v_rows(j - 1)

            def gated_ready(first):
                def ready(k):
                    pe.wait_ge(a_hi_done, 32 + first + k + 1)
                    pe.wait_ge(a_lo_done, 32 + first + k + 1)
                return ready

            u_half(0, J_U0)
            out_product(J_CMO0, gated_ready(0))
            u_half(8, J_U1)
            out_product(J_CMO1, gated_ready(8))
            mlp(3, J_MLP1)

            out_tr(KT - 1)
            pe.wait_ge(ty_evac, 8)
            pe.wait_ge(ssum_added, 35)
            for c in range(NC):
                pe.matmul(ps[:, 4, c:c + 1], ssum[:, c * CH:(c + 1) * CH], ones[:, 0:1], start=True, stop=True)
            pe.matmul(ps[0:NS, 5, 0:1], ssum[:, TP:T], ones[:, 0:1], start=True, stop=True).then_inc(fin_stat, 1)

        @block.scalar
        def _(act_e):
            def split_w(pair):
                act_e.wait_ge(w_landed[pair.slot], pair.use(1) * 16)
                if due(c_columns(pair)):
                    act_e.wait_ge(c_landed, c_columns(pair))
                if due(pair.s - 1):
                    act_e.wait_ge(unit_done, Pair(pair.s - 2, pair.loop).multiplied())
                w = slice(0, P if pair.s == J_DT and isinstance(pair.loop, int) else 256)
                k = slice(0, pair.tiles())
                nc.scalar.activation(w_hi[:, pair.slot, k, w], w32[:, pair.slot, k, w], ACT.Copy)\
                  .then_inc(w_hi_done, 1)

            def square(n, m, x_final):
                x_final(m)
                if m == 0:
                    if due(n):
                        act_e.wait_ge(r_ready, n)
                    if n == 1:
                        act_e.wait_ge(y_lo_done, 16)
                    if n == 3:
                        act_e.wait_ge(vrec_done, 2)
                        act_e.wait_ge(a_lo_done, 48)
                    dst = ssum[:, :]
                else:
                    if due(7 * n + m - 2):
                        act_e.wait_ge(ssum_added, 7 * n + m - 2)
                    dst = sq[:, m % 2, :]
                nc.scalar.activation(dst, xT[:, m, :], ACT.Square).then_inc(sq_ready, 1)

            def make_h(n, m, gain, x_final, read_out):
                x_final(m)
                if due(read_out):
                    act_e.wait_ge(unit_done, read_out)
                nc.scalar.activation(h_hi[:, m, :], xT[:, m, :], ACT.Copy, scale=feat[:, gain + m:gain + m + 1])\
                  .then_inc(h_hi_ready, 1)
                square(n, m, x_final)

            def root(n):
                act_e.wait_ge(stats_done, n + 1)
                nc.scalar.activation(halves(ssum[:, :]), ps[:, 4:6, 0:TH], ACT.Sqrt, bias=eps[:, 0:1], scale=1.0 / D)\
                  .then_inc(root_done, 1)

            act_e.dma_start(xs_row[:, :], x_sample.rearrange("b s d -> (b s) d")).then_inc(xs_landed, 16)
            r0 = 0
            for src in (norm_mix_g.rearrange("l (t c) -> (l t) c", c=P), norm_mlp_g.rearrange("l (t c) -> (l t) c", c=P),
                        norm_final_g.rearrange("(t c) -> t c", c=P), ssd_norm_g[0].rearrange("(t c) -> t c", c=P),
                        cm_b_in[0].rearrange("(t c) -> t c", c=P), cm_v_norm_g[0].rearrange("(t c) -> t c", c=P)):
                act_e.dma_start(frow[r0:r0 + src.shape[0], :], src).then_inc(frow_landed, 16)
                r0 += src.shape[0]
            r0 = 0
            by_group = crow.rearrange("r (g t) c -> r g t c", t=4)
            for src in (ssd_conv_w[0], ssd_conv_b[0:1], state_conv[0].rearrange("b k c -> (b k) c")):
                n = src.shape[0]
                for i in range(2):
                    act_e.dma_start(by_group[r0:r0 + n, :, i, :],
                                    src[:, DI + i * GROUPS * N:DI + (i + 1) * GROUPS * N].rearrange("r (g c) -> r g c", c=P))\
                         .then_inc(crow_landed, 16)
                act_e.dma_start(by_group[r0:r0 + n, :, 2:4, :],
                                src[:, 0:DI].rearrange("r (g t c) -> r g t c", t=2, c=P)).then_inc(crow_landed, 16)
                r0 += n
            act_e.dma_start(conv_sample[0, :, 0:2, :], state_conv[0, :, 1:3, :]).then_inc(conv_old, 16)

            def x_prologue(m):
                act_e.wait_ge(x_ready, m + 1)
                act_e.wait_ge(xs_ready, 1)

            act_e.wait_ge(feat_ready, 1)
            for m in range(KT):
                make_h(0, m, G_MIX, x_prologue, 0)
            split_w(Pair(J_DT))
            split_w(Pair(1))
            act_e.wait_ge(const_ready, 2)
            root(0)
            split_w(Pair(2))

            def fill(g, t):
                k = 4 * g + t
                if due(k - 1):
                    act_e.wait_ge(tap0_done, k - 1)
                if due(3 * (k - 1)):
                    act_e.wait_ge(tap_done, 3 * (k - 1))
                if due(k - 1):
                    act_e.wait_ge(cst_tr, k - 1)
                if k < 2:
                    act_e.wait_ge(convf_ready, 2)
                    act_e.wait_ge(raw_zeroed, 1)
                nc.scalar.activation(raw[:, t % 2, S0:RAW].rearrange("p (b k) -> p b k", k=TAPS)[:, :, 0:3],
                                     convf[:, k, 5:CW].rearrange("p (b k) -> p b k", k=3), ACT.Copy)\
                  .then_inc(sraw_filled, 1)

            def tap0(g, t):
                k = 4 * g + t
                act_e.wait_ge(evac_done, Pair(group_pair(g, t // 2)).unit(t % 2, 1))
                act_e.wait_ge(sraw_filled, k + 1)
                if due(2 * g - 2):
                    act_e.wait_ge(yoff_done, 2 * g - 2)
                    act_e.wait_ge(comb_done, 2 * g - 2)
                if due(g - 1):
                    act_e.wait_ge(xdts_done, g - 1)
                nc.scalar.activation(act[:, g % 2, t, :], raw[:, t % 2, 0:CONV_N], ACT.Identity,
                                     bias=convf[:, k, 4:5], scale=convf[:, k, 0:1]).then_inc(tap0_done, 1)

            def silu(g, t):
                act_e.wait_ge(tap_done, 3 * (4 * g + t + 1))
                nc.scalar.activation(act[:, g % 2, t, :], act[:, g % 2, t, :], ACT.Silu).then_inc(silu_done, 1)

            def silu_z(g, i):
                act_e.wait_ge(evac_done, Pair(group_pair(g, 2)).unit(i, 1))
                nc.scalar.activation(zs[:, i, :], zs[:, i, :], ACT.Silu).then_inc(z_silu_done, 1)

            def cst(g):
                act_e.wait_ge(cst_tr, 4 * g + 4)
                if due(64 * g):
                    act_e.wait_ge(cst_out, 64 * g)
                nc.scalar.activation(cstage[:, :, :], ps[0:35, 7, :].rearrange("p (t c) -> p t c", c=P), ACT.Copy)\
                  .then_inc(cst_evac, 1)

            def y_squares(g):
                if g < 0:
                    return
                for i, dst in ((0, ssum[:, :]), (1, sq[:, 0, :])):
                    act_e.wait_ge(comb_done, 2 * g + i + 1)
                    if due(g):
                        act_e.wait_ge(ysum_done, g)
                    if due(2 * g):
                        act_e.wait_ge(ynorm_done, 2 * g)
                    act_e.wait_ge(r_ready, 1)
                    nc.scalar.activation(dst, work[:, i, :], ACT.Square).then_inc(ysq_done, 1)

            def y_root(g):
                if g < 0:
                    return
                act_e.wait_ge(rms_done, g + 1)
                nc.scalar.activation(halves(ssum[:, :]), ps[:, 6:8, 0:TH], ACT.Sqrt, bias=eps[:, 0:1], scale=1.0 / 256)\
                  .then_inc(yroot_done, 1)

            def y_high(g):
                if g < 0:
                    return
                for i in range(2):
                    act_e.wait_ge(ynorm_done, 2 * g + i + 1)
                    if g >= 4:
                        act_e.wait_ge(unit_done, Pair(J_OUT0 + 3).unit(1, 1))
                    nc.scalar.activation(a_hi[:, (2 * g + i) % 8, :], work[:, i, :], ACT.Copy).then_inc(y_hi_done, 1)

            def state_evac(g):
                if g < 0:
                    return
                act_e.wait_ge(h4_tr, g + 1)
                if due(32 * g):
                    act_e.wait_ge(ssm_out, 32 * g)
                nc.scalar.activation(ssm_stage[:, :, :], ps[:, 5, 256:512].rearrange("p (i n) -> p i n", i=2), ACT.Copy)\
                  .then_inc(h4_evac, 1)

            def abc_load(g, i):
                if i == 0:
                    if due(2 * g):
                        act_e.wait_ge(comb_done, 2 * g)
                elif due(2 * g):
                    act_e.wait_ge(ydiag_done, 2 * g)
                act_e.dma_start(abc[:, i], scr_a[4 * g + 2 * i:4 * g + 2 * i + 2, :].partition_broadcast(P))\
                     .then_inc(abc_landed[i], 16)

            def exp_m(g, i):
                act_e.wait_ge(abc_landed[i], 16 * (g + 1))
                for hh in range(2):
                    h = 4 * g + 2 * i + hh
                    for c in range(NC):
                        part = abc[:, i, hh, c * CH:(c + 1) * CH]
                        ins = nc.scalar.activation(part, part, ACT.Relu, bias=tokS[:, 2, c, h:h + 1], scale=-1.0)
                    ins.then_inc(seg_done, 1)
                for hh in range(2):
                    act_e.wait_ge(seg_done, 4 * g + 2 * (1 - i) + hh + 1)
                    nc.scalar.activation(abc[:, i, hh, :], abc[:, i, hh, :], ACT.Exp, scale=-1.0).then_inc(exp_done, 1)

            def ef(g):
                act_e.wait_ge(ydiag_done, 2 * g + 1)
                for i in range(2):
                    for hh in range(2):
                        act_e.dma_start(abc[hh * HD:(hh + 1) * HD, 0, i, :],
                                        scr_a[4 * g + 2 * i + hh, :].partition_broadcast(HD)).then_inc(ef_landed, 16)

            def ef_exp(g):
                act_e.wait_ge(ef_landed, 64 * (g + 1))
                for i in range(2):
                    nc.scalar.activation(abc[:, 0, i, :], abc[:, 0, i, :], ACT.Exp).then_inc(ef_done, 1)

            def window(g):
                nxt = g + 1
                more = nxt < GROUPS
                split_w(Pair(group_pair(g, 2) + 1))
                exp_m(g, 1)
                y_squares(g - 1)
                abc_load(g, 0)
                silu(g, 2)
                silu(g, 3)
                cst(g)
                act_e.wait_ge(bc_tr, g + 1)
                if due(16 * g):
                    act_e.wait_ge(bc_out, 16 * g)
                nc.scalar.activation(bcrow[:, :], ps[0:NS, 5, 0:2 * N], ACT.Copy).then_inc(bc_evac, 1)
                state_evac(g - 1)
                silu_z(g, 0)
                exp_m(g, 0)
                y_root(g - 1)
                silu_z(g, 1)
                if more:
                    fill(nxt, 0)
                    fill(nxt, 1)
                split_w(Pair(group_pair(nxt, 1) if more else J_OUT1 + 1))
                y_high(g - 1)
                if more:
                    tap0(nxt, 0)
                act_e.wait_ge(Btr_done, g + 1)
                if due(4 * g):
                    act_e.wait_ge(st_done, 4 * g)
                nc.scalar.activation(Btok[:, :, :], ps[:, 6, :].rearrange("p (c n) -> p c n", n=N), ACT.Copy)\
                  .then_inc(Btok_done, 1)
                ef(g)
                if more:
                    tap0(nxt, 1)
                    fill(nxt, 2)
                split_w(Pair(group_pair(nxt, 1) + 1 if more else J_OUT1 + 2))
                if more:
                    silu(nxt, 0)
                    silu(nxt, 1)
                    tap0(nxt, 2)
                    fill(nxt, 3)
                ef_exp(g)
                if more:
                    abc_load(nxt, 1)
                    tap0(nxt, 3)

            act_e.wait_ge(crow_done, 2)
            for i, src in ((0, ssd_dt_bias), (1, ssd_a_log), (2, ssd_d)):
                act_e.dma_start(dt_par[:, i:i + 1], src[0].rearrange("(h o) -> h o", o=1)).then_inc(par_landed, 16)
            act_e.wait_ge(par_landed, 48)
            nc.scalar.activation(dt_par[:, 1:2], dt_par[:, 1:2], ACT.Exp).then_inc(dt_act_done, 1)
            act_e.wait_ge(dt_vec_done, 1)
            nc.scalar.activation(dt_e[:, :], dt_v[:, :], ACT.Abs).then_inc(dt_act_done, 1)
            act_e.wait_ge(dt_act_done, 2)
            nc.scalar.activation(dt_e[:, :], dt_e[:, :], ACT.Exp, scale=-1.0).then_inc(dt_act_done, 1)
            act_e.wait_ge(dt_act_done, 3)
            nc.scalar.activation(dt_e[:, :], dt_e[:, :], ACT.Ln, bias=ones[0:HEADS, 0:1]).then_inc(dt_act_done, 1)
            for c in range(NC):
                act_e.wait_ge(dt_vec_done, 5 + c)
                nc.scalar.activation(dt_end[:, c, :], dt_a[:, c * CH:(c + 1) * CH], ACT.Exp,
                                     bias=dt_a[:, (c + 1) * CH - 1:(c + 1) * CH], scale=-1.0).then_inc(dt_act_done, 1)
            nc.scalar.activation(dt_small[:, 8:16], dt_v[:, TP:T], ACT.Exp).then_inc(dt_act_done, 1)
            nc.scalar.activation(dt_small[:, 20:24], dt_a[:, CH - 1:TP:CH], ACT.Exp).then_inc(dt_act_done, 1)
            act_e.wait_ge(dt_vec_done, 9)
            act_e.wait_ge(dt_act_done, 10)
            act_e.dma_start(scr_a, dt_a[:, 0:TP]).then_inc(scr_a_done, 16)
            act_e.dma_start(scr_s, dt_small[:, :]).then_inc(scr_s_done, 16)

            fill(0, 0)
            fill(0, 1)
            tap0(0, 0)
            tap0(0, 1)
            act_e.wait_ge(scr_s_done, 16)
            for hh in range(2):
                act_e.dma_start(dtf[hh * HD:(hh + 1) * HD, :, :], scr_s[hh:HEADS:2, 0:20].partition_broadcast(HD))\
                     .then_inc(dtf_landed, 16)
            act_e.dma_start(cdec[:, :, :], scr_s[:, 20:24].partition_broadcast(P)).then_inc(cdec_landed, 16)
            act_e.wait_ge(scr_a_done, 16)
            silu(0, 0)
            silu(0, 1)
            fill(0, 2)
            tap0(0, 2)
            fill(0, 3)
            split_w(Pair(3))
            act_e.wait_ge(dt_tok_done, 1)
            act_e.wait_ge(dtf_landed, 32)
            abc_load(0, 1)
            tap0(0, 3)
            for g in range(5):
                window(g)
            for i in range(4):
                split_w(Pair(J_OUT0 + i + 1))
            for g in range(5, GROUPS):
                window(g)
            split_w(Pair(J_OUT1 + 3))
            y_squares(7)
            split_w(Pair(J_TAIL))
            y_root(7)
            y_high(7)
            state_evac(7)

            def x_after(pair0):
                def ready(m):
                    act_e.wait_ge(evac_done, Pair(pair0.s + m // 2, pair0.loop).unit(m % 2, 1))
                return ready

            def out_with_h(n, J, gain, read_out):
                for i in range(4):
                    split_w(Pair(J + i + 1))
                    for half in range(2):
                        make_h(n, 2 * i + half, gain, x_after(Pair(J)), read_out)

            def tail_added(m):
                act_e.wait_ge(evac_done, Pair(J_TAIL).unit(0, m + 1))

            split_w(Pair(J_MLP0))
            for m in range(KT):
                make_h(1, m, G_MLP, tail_added, Pair(group_pair(7, 2)).unit(1, 1))

            def mlp(n, J, last):
                base = 0 if n == 1 else 48

                def chunk(c, first, final):
                    for i in range(4):
                        split_w(Pair(J + i + 1, c * 4))
                        if first and i == 0:
                            root(n)
                        for half in range(2):
                            j = 2 * i + half
                            act_e.wait_ge(a32_done, c * 8 + (base + j + 1))
                            if first and i == half == 0:
                                act_e.wait_ge(unit_done, Pair(J - 1).multiplied())
                            elif not first:
                                act_e.wait_ge(unit_done, Pair(J + i, c * 4).unit(half, 0))
                            nc.scalar.activation(a_hi[:, j, :], work[:, half, :], ACT.Copy).then_inc(a_hi_done, 1)
                    for i in range(4):
                        if not (final and last and i == 3):
                            split_w(Pair(J + 4 + i + 1, c * 4))
                        if final:
                            for half in range(2):
                                m = 2 * i + half
                                up_done = Pair(J + 3, c * 4).unit(1, 1)
                                if last:
                                    final_tile(m)
                                else:
                                    make_h(n + 1, m, G_MIX + KT, x_after(Pair(J + 4, c * 4)), up_done)

                def final_tile(m):
                    square(4, m, x_after(Pair(J + 4 + 8 * (CHUNKS - 1))))

                chunk(0, True, False)
                with act_e.Fori(1, CHUNKS - 1) as c:
                    chunk(c, False, False)
                chunk(CHUNKS - 1, False, True)

            mlp(1, J_MLP0, False)

            act_e.wait_ge(sstored[0], 32 * 16)
            act_e.wait_ge(sstored[1], 32 * 16)
            act_e.wait_ge(ssm_out, 32 * 7)
            act_e.wait_ge(last_ssm_out, 32)
            act_e.wait_ge(cst_out, 64 * 8)
            for i in range(8):
                split_w(Pair(J_V + i + 1))
                if i == 0:
                    root(2)
                for half in range(2):
                    j = 2 * i + half
                    act_e.wait_ge(evac_done, Pair(J_V + i).unit(half, 1))
                    if due(j - 1):
                        act_e.wait_ge(v_tr, j - 1)
                        act_e.wait_ge(vsmp_done, j - 1)
                    nc.scalar.activation(gv[:, j % 2, :], work[:, j % 2, :], ACT.Gelu,
                                         bias=feat[:, B_CM + 16 + j:B_CM + 17 + j]).then_inc(gelu_done, 1)
                    act_e.wait_ge(gelu_done, j + 1)
                    if j == 0:
                        act_e.wait_ge(r_ready, 3)
                    else:
                        if due(j - 2):
                            act_e.wait_ge(vsum_done, j - 2)
                    nc.scalar.activation(ssum[:, :] if j == 0 else sq[:, j % 2, :], gv[:, j % 2, :], ACT.Square)\
                      .then_inc(vsq_done, 1)

            def u_half(first, J):
                for i in range(4):
                    split_w(Pair(J + i + 1))
                    for half in range(2):
                        j = first + 2 * i + half
                        act_e.wait_ge(evac_done, Pair(J + i).unit(half, 1))
                        nc.scalar.activation(work[:, j % 2, :], work[:, j % 2, :], ACT.Gelu,
                                             bias=feat[:, B_CM + j:B_CM + 1 + j]).then_inc(gelu_done, 1)
                        if j == 0:
                            act_e.wait_ge(vstat_done, 1)
                            nc.scalar.activation(r_tok[:, 0:NC], ps[:, 4, 0:NC], ACT.Sqrt, bias=eps[:, 0:1],
                                                 scale=1.0 / CMW).then_inc(vroot_done, 1)
                            nc.scalar.activation(r_smp[:, :], ps[:, 4, 8:8 + NS], ACT.Sqrt, bias=eps[:, 0:1],
                                                 scale=1.0 / CMW).then_inc(vroot_done, 1)
                            act_e.wait_ge(vrec_done, 2)
                            act_e.wait_ge(vtok_done, 16)
                            for c in range(2, NC):
                                nc.scalar.activation(vtok[:, c, :], vtok[:, c, :], ACT.Copy, scale=r_tok[:, c:c + 1])\
                                  .then_inc(vscaled_act, 1)
                        act_e.wait_ge(a32_done, 32 + j + 1)
                        act_e.wait_ge(unit_done, Pair(J_MLP0 + 31).unit(1, 1) if first == 0 else Pair(J_CMO0 + 3).unit(1, 1))
                        nc.scalar.activation(a_hi[:, j % 8, :], sq[:, j % 2, :], ACT.Copy).then_inc(a_hi_done, 1)

            u_half(0, J_U0)
            for i in range(4):
                split_w(Pair(J_CMO0 + i + 1))
            u_half(8, J_U1)
            out_with_h(3, J_CMO1, G_MLP + KT, Pair(J_CMO1 - 1).unit(1, 1))
            mlp(3, J_MLP1, True)
            act_e.wait_ge(fin_stat, 1)
            nc.scalar.activation(r_fin[:, 0:NC], ps[:, 4, 0:NC], ACT.Sqrt, bias=eps[:, 0:1], scale=1.0 / D)\
              .then_inc(fin_root, 1)
            nc.scalar.activation(r_fin[0:NS, NC:NC + 1], ps[0:NS, 5, 0:1], ACT.Sqrt, bias=eps[0:NS, 0:1], scale=1.0 / D)\
              .then_inc(fin_root, 1)
            act_e.wait_ge(fin_rec, 2)
            act_e.wait_ge(ty_evac, 9)
            for c in range(1, NC, 2):
                nc.scalar.activation(ytok[:, c, :], ytok[:, c, :], ACT.Copy, scale=r_fin[:, c:c + 1])\
                  .then_inc(y_scaled_act, 1)

        @block.gpsimd
        def _(pool):
            nc.gpsimd.memset(ident[:, :], 1.0).then_inc(ident_ready, 1)
            nc.gpsimd.memset(causal[:, :], 1.0).then_inc(ident_ready, 1)
            pool.wait_ge(ident_ready, 2)
            nc.gpsimd.affine_select(out=ident[:, :], in_=ident[:, :], compare_op=ALU.is_equal, fill=0.0, base=0,
                                    pattern=[[-1, P]], channel_multiplier=1).then_inc(ident_ready, 1)
            nc.gpsimd.affine_select(out=causal[:, :], in_=causal[:, :], compare_op=ALU.is_ge, fill=0.0, base=0,
                                    pattern=[[1, P]], channel_multiplier=-1).then_inc(ident_ready, 1)
            nc.gpsimd.memset(w32[:, 0, :, HEADS:P], 0.0).then_inc(w_cleared, 1)
            nc.gpsimd.memset(ones[:, :], 1.0).then_inc(const_ready, 1)
            nc.gpsimd.memset(eps[:, :], EPS).then_inc(const_ready, 1)

            def add_squares(n):
                for m in range(1, KT):
                    pool.wait_ge(sq_ready, 8 * n + m + 1)
                    if due(7 * n + m - 1):
                        pool.wait_ge(ssum_added, 7 * n + m - 1)
                    nc.gpsimd.tensor_tensor(ssum[:, :], ssum[:, :], sq[:, m % 2, :], ALU.add).then_inc(ssum_added, 1)

            add_squares(0)
            pool.wait_ge(crow_done, 2)
            pool.wait_ge(x_ready, 8)
            pool.wait_ge(xt_done, 8)
            nc.gpsimd.memset(dt_one[:, :], 1.0).then_inc(const_ready, 1)
            nc.gpsimd.memset(dt_small[:, :], 0.0).then_inc(const_ready, 1)
            nc.gpsimd.memset(raw[:, :, 0:TAPS - 1], 0.0).then_inc(raw_zeroed, 1)

            def y_sum(g):
                if g < 0:
                    return
                pool.wait_ge(ysq_done, 2 * g + 2)
                nc.gpsimd.tensor_tensor(ssum[:, :], ssum[:, :], sq[:, 0, :], ALU.add).then_inc(ysum_done, 1)

            def y_low(g):
                if g < 0:
                    return
                for i in range(2):
                    pool.wait_ge(y_hi_done, 2 * g + i + 1)
                    pool.wait_ge(ynorm_done, 2 * g + i + 1)
                    k = (2 * g + i) % 8
                    nc.gpsimd.tensor_tensor(a_lo[:, k, :], work[:, i, :], a_hi[:, k, :].bitcast(F32), ALU.subtract)\
                      .then_inc(y_lo_done, 1)

            def by_tile(dram, n):
                g, b = n // 4, 2 * (n % 4)
                return [dram[0, b:b + 2, 4 * g + 2 * i:4 * g + 2 * i + 2].rearrange("b h p n -> (h p) b n")
                        for i in range(2)]

            def load_states(n):
                if due(n - 1):
                    pool.wait_ge(smul_done, n - 1)
                if due(32 * (n // 2)):
                    pool.wait_ge(sstored[n % 2], 32 * (n // 2))
                for i, src in enumerate(by_tile(state_ssm, n)):
                    pool.dma_start(hst[:, n % 2, 2 * i:2 * i + 2, :], src).then_inc(hst_landed[n % 2], 16)

            def load_bc(n):
                if due(n - 1):
                    pool.wait_ge(smul_done, n - 1)
                    pool.wait_ge(state_added, 2 * (n - 1))
                pool.dma_start(bcs[:, n % 2], scr_bc[n // 4, 2 * (n % 4):2 * (n % 4) + 2, :].partition_broadcast(P))\
                    .then_inc(bcs_landed[n % 2], 16)

            def window(g):
                y_sum(g - 1)
                if g == 0:
                    load_states(0)
                load_states(4 * g + 1)
                pool.wait_ge(bc_evac, g + 1)
                pool.dma_start(scr_bc[g], bcrow[:, :]).then_inc(bc_out, 16)
                pool.wait_ge(bc_out, 16 * (g + 1))
                load_bc(4 * g)
                load_bc(4 * g + 1)
                pool.wait_ge(xdts_done, g + 1)
                for n in range(4 * g, 4 * g + 4):
                    b0 = 2 * (n % 4)
                    state = hst[:, n % 2]
                    pool.wait_ge(hst_landed[n % 2], 32 * (n // 2 + 1))
                    nc.gpsimd.tensor_tensor(state.rearrange("p (i b) n -> p i b n", i=2),
                                            state.rearrange("p (i b) n -> p i b n", i=2),
                                            dtf[:, 2 * g:2 * g + 2, 8 + b0:10 + b0].unsqueeze(3).broadcast_to([P, 2, 2, N]),
                                            ALU.mult).then_inc(decay_done, 1)
                    pool.wait_ge(bcs_landed[n % 2], 16 * (n // 2 + 1))
                    pool.wait_ge(decay_done, n + 1)
                    for i in range(2):
                        k = 2 * n + i
                        if due(k):
                            pool.wait_ge(state_added, k)
                        nc.gpsimd.tensor_tensor(outer[:, :, :], bcs[:, n % 2, :, 0:N],
                                                xdts[:, i, b0:b0 + 2].unsqueeze(2).broadcast_to([P, 2, N]), ALU.mult)\
                          .then_inc(outer_done, 1)
                        pool.wait_ge(outer_done, k + 1)
                        nc.gpsimd.tensor_tensor(state[:, 2 * i:2 * i + 2, :], state[:, 2 * i:2 * i + 2, :], outer[:, :, :],
                                                ALU.add).then_inc(state_added, 1)
                    pool.wait_ge(state_added, 2 * n + 2)
                    for i, dst in enumerate(by_tile(ssm_sample, n)):
                        pool.dma_start(dst, state[:, 2 * i:2 * i + 2, :]).then_inc(sstored[n % 2], 16)
                    if n % 4 == 0 and g < GROUPS - 1:
                        y_low(g - 1)
                    if n % 4 in (1, 2):
                        load_bc(n + 1)
                    if n % 4 and n + 1 < 4 * GROUPS:
                        load_states(n + 1)

            for g in range(GROUPS):
                window(g)
            y_sum(7)
            pool.wait_ge(h4_evac, 8)
            for i in range(2):
                pool.dma_start(ssm_prompt[0, 0, 28 + 2 * i:30 + 2 * i].rearrange("h p n -> (h p) n"), ssm_stage[:, i, :])\
                    .then_inc(last_ssm_out, 16)
            add_squares(1)
            add_squares(2)
            pool.wait_ge(sq_ready, 17)
            pool.wait_ge(sstored[0], 32 * 16)
            pool.wait_ge(sstored[1], 32 * 16)
            pool.wait_ge(ssm_out, 32 * 7)
            pool.wait_ge(last_ssm_out, 32)
            pool.wait_ge(cst_out, 64 * 8)
            pool.dma_start(wmix[:, :, :], cm_w_s[0].rearrange("g t s -> t g s")).then_inc(mix_landed, 16)
            pool.dma_start(bmix[:, :, :], cm_b_s[0].partition_broadcast(P)).then_inc(b_landed, 16)
            pool.dma_start(w00[:, :, :], cm_w_s[0, :, 0, 0:2].partition_broadcast(P)).then_inc(b_landed, 16)
            for j in range(16):
                pool.wait_ge(gelu_done, j + 1)
                nc.gpsimd.tensor_copy(vsmp[:, j, :], gv[:, j % 2, TP:T]).then_inc(vsmp_done, 1)
                if j:
                    pool.wait_ge(vsq_done, j + 1)
                    if due(j - 1):
                        pool.wait_ge(vsum_done, j - 1)
                    nc.gpsimd.tensor_tensor(ssum[:, :], ssum[:, :], sq[:, j % 2, :], ALU.add).then_inc(vsum_done, 1)
            for n in range(4):
                pool.wait_ge(vs_evac, n + 1)
                pool.dma_start(cm_v_sample[0, :, 0, n * 512:(n + 1) * 512], vs_row[:, :, :].rearrange("p a b -> p (a b)"))\
                    .then_inc(vs_out, 16)
            add_squares(3)
            add_squares(4)
            pool.wait_ge(out_done, 80)
            pool.wait_ge(conv_old, 16)
            pool.wait_ge(cst_out, 64 * 8)
            pool.wait_ge(ssm_out, 32 * 7)
            pool.wait_ge(last_ssm_out, 32)
            pool.wait_ge(sstored[0], 32 * 16)
            pool.wait_ge(sstored[1], 32 * 16)
            pool.wait_ge(vs_out, 64)

        @block.vector
        def _(dve):
            def split_w(pair):
                dve.wait_ge(w_hi_done, pair.times(1, 1))
                dve.wait_ge(w_landed[pair.slot], pair.use(1) * 16)
                if due(c_columns(pair)):
                    dve.wait_ge(c_landed, c_columns(pair))
                if due(pair.s - 1):
                    dve.wait_ge(unit_done, Pair(pair.s - 2, pair.loop).multiplied())
                w = slice(0, P if pair.s == J_DT and isinstance(pair.loop, int) else 256)
                k = slice(0, pair.tiles())
                nc.vector.tensor_tensor(w_lo[:, pair.slot, k, w], w32[:, pair.slot, k, w],
                                        w_hi[:, pair.slot, k, w].bitcast(F32), ALU.subtract).then_inc(w_lo_done, 1)

            def evac_scaled(pair, half, dst, n=HEADS * 4):
                dve.wait_ge(unit_done, pair.unit(half, 1))
                nc.vector.tensor_tensor(halves(dst), psum_tok(1 - half)[0:n], halves(rstd[0:n, :]), ALU.mult)\
                  .then_inc(evac_done, 1)

            def evac_added(pair, half, m):
                dve.wait_ge(unit_done, pair.unit(half, 1))
                nc.vector.tensor_tensor(halves(xT[:, m, :]), psum_tok(1 - half), halves(xT[:, m, :]), ALU.add)\
                  .then_inc(evac_done, 1)

            def h_low(n, m, gain):
                dve.wait_ge(h_hi_ready, 8 * n + m + 1)
                nc.vector.scalar_tensor_tensor(out=h_lo[:, m, :], in0=xT[:, m, :], scalar=feat[:, gain + m:gain + m + 1],
                                               in1=h_hi[:, m, :].bitcast(F32), op0=ALU.mult, op1=ALU.subtract)\
                  .then_inc(h_lo_ready, 1)

            def inv_rms(n):
                dve.wait_ge(root_done, n + 1)
                nc.vector.reciprocal(rstd[:, :], ssum[:, :]).then_inc(r_ready, 1)
                dve.wait_ge(r_ready, n + 1)

            for m in range(KT):
                dve.wait_ge(xt_done, m + 1)
                nc.vector.tensor_copy(xT[:, m, 0:TP], ps[:, 4 + m % 2, :]).then_inc(x_ready, 1)
                if m == 0:
                    dve.wait_ge(frow_done, 1)
                    nc.vector.tensor_copy(xT[:, :, TP:T], ps[:, 6, 0:KT * NS].rearrange("p (k b) -> p k b", k=KT))\
                      .then_inc(xs_ready, 1)
                    nc.vector.tensor_copy(feat[:, :], ps[:, 6, 128:128 + FEAT]).then_inc(feat_ready, 1)
                    dve.wait_ge(feat_ready, 1)
                    dve.wait_ge(xs_ready, 1)
                if m:
                    h_low(0, m - 1, G_MIX)
            h_low(0, KT - 1, G_MIX)
            split_w(Pair(J_DT))
            split_w(Pair(1))
            for half in range(2):
                dve.wait_ge(crow_done, half + 1)
                nc.vector.tensor_copy(convf[:, 16 * half:16 * half + 16, :],
                                      ps[:, 6 + half, 0:16 * CW].rearrange("p (t c) -> p t c", c=CW))\
                  .then_inc(convf_ready, 1)
            inv_rms(0)

            def evac_unit(g, t):
                if g == GROUPS:
                    evac_added(Pair(J_OUT1 + t // 2), t % 2, t)
                    return
                pair, half = Pair(group_pair(g, t // 2)), t % 2
                if t >= 4:
                    if due(2 * g - 5 + t):
                        dve.wait_ge(comb_done, 2 * g - 5 + t)
                    evac_scaled(pair, half, zs[:, t - 4, :])
                    return
                k = 4 * g + t
                slot = 1 - half
                dve.wait_ge(unit_done, pair.unit(half, 1))
                if due(k - 1):
                    dve.wait_ge(tap0_done, k - 1)
                    dve.wait_ge(cst_tr, k - 1)
                if due(3 * (k - 1)):
                    dve.wait_ge(tap_done, 3 * (k - 1))
                nc.vector.tensor_tensor(raw[:, t % 2, S0 + TAPS - 1:RAW:TAPS], ps[:, 2 * slot + 1, 256:256 + NS],
                                        rstd[:, TP:T], ALU.mult).then_inc(new_evac, 1)
                nc.vector.tensor_tensor(halves(raw[:, t % 2, TAPS - 1:TAPS - 1 + TP]), ps[:, 2 * slot:2 * slot + 2, 0:256],
                                        halves(rstd[:, 0:TP]), ALU.mult).then_inc(evac_done, 1)

            def conv(g, t):
                k = 4 * g + t
                dve.wait_ge(tap0_done, k + 1)
                dve.wait_ge(new_evac, k + 1)
                dve.wait_ge(evac_done, Pair(group_pair(g, t // 2)).unit(t % 2, 1))
                for tap in range(1, TAPS):
                    if due(3 * k + tap - 1):
                        dve.wait_ge(tap_done, 3 * k + tap - 1)
                    nc.vector.scalar_tensor_tensor(out=act[:, g % 2, t, :], in0=raw[:, t % 2, tap:tap + CONV_N],
                                                   scalar=convf[:, k, tap:tap + 1], in1=act[:, g % 2, t, :],
                                                   op0=ALU.mult, op1=ALU.add).then_inc(tap_done, 1)

            def y_norm(g):
                if g < 0:
                    return
                dve.wait_ge(yroot_done, g + 1)
                nc.vector.reciprocal(ssum[:, :], ssum[:, :]).then_inc(yr_done, 1)
                dve.wait_ge(yr_done, g + 1)
                for i in range(2):
                    nc.vector.scalar_tensor_tensor(out=work[:, i, :], in0=work[:, i, :],
                                                   scalar=feat[:, G_SSD + 2 * g + i:G_SSD + 2 * g + i + 1],
                                                   in1=ssum[:, :], op0=ALU.mult, op1=ALU.mult).then_inc(ynorm_done, 1)

            def y_low(g):
                if g < 0:
                    return
                for i in range(2):
                    dve.wait_ge(y_hi_done, 2 * g + i + 1)
                    dve.wait_ge(ynorm_done, 2 * g + i + 1)
                    k = (2 * g + i) % 8
                    nc.vector.tensor_tensor(a_lo[:, k, :], work[:, i, :], a_hi[:, k, :].bitcast(F32), ALU.subtract)\
                      .then_inc(y_lo_done, 1)

            def decayed(g, i):
                for hh in range(2):
                    dve.wait_ge(exp_done, 4 * g + (2 if i == 0 else 0) + hh + 1)
                    dve.wait_ge(cbm_done, g + 1)
                    nc.vector.tensor_tensor(abc[:, i, hh, :], abc[:, i, hh, :], cbm[:, :, :].rearrange("p c q -> p (c q)"),
                                            ALU.mult).then_inc(m_done, 1)

            def sample(g, n):
                k, b0 = 4 * g + n, 2 * n
                prod = sq[:, 1, 0:4 * N].rearrange("p (i b n) -> p i b n", i=2, b=2)
                dve.wait_ge(state_added, 2 * k + 2)
                if due(k):
                    dve.wait_ge(sred_done, k)
                if k == 0:
                    dve.wait_ge(ssum_added, 7)
                nc.vector.tensor_tensor(prod, hst[:, k % 2].rearrange("p (i b) n -> p i b n", i=2),
                                        bcs[:, k % 2, :, N:2 * N].unsqueeze(1).broadcast_to([P, 2, 2, N]), ALU.mult)\
                  .then_inc(smul_done, 1)
                dve.wait_ge(smul_done, k + 1)
                nc.vector.tensor_reduce(ysmp[:, :, b0:b0 + 2], prod, AX.X, ALU.add).then_inc(sred_done, 1)

            def y_diag(g, i):
                dve.wait_ge(ydiag_done, 2 * g + i + 1)
                if due(2 * g):
                    dve.wait_ge(y_hi_done, 2 * g)
                    dve.wait_ge(y_lo_done, 2 * g)
                nc.vector.scalar_tensor_tensor(out=work[:, i, 0:TP], in0=act[:, g % 2, 2 + i, 0:TP],
                                               scalar=dtf[:, 2 * g + i, 16:17], in1=ps[:, 4 + i, :],
                                               op0=ALU.mult, op1=ALU.add).then_inc(y1_done, 1)

            def by_head(ap):
                return ap.rearrange("p (h d) -> p h d", d=HD)

            def states(g):
                if due(2 * g):
                    dve.wait_ge(yoff_done, 2 * g)
                if due(g):
                    dve.wait_ge(h4_tr, g)
                for c in range(NC):
                    bank = ps[:, 6 if c < 2 else 4, (c % 2) * 256:(c % 2) * 256 + 256]
                    dve.wait_ge(st_done, 4 * g + (2 if c < 2 else 4))
                    if c == 0:
                        nc.vector.tensor_copy(hprev[:, 0, :], bank).then_inc(hstep_done, 1)
                        continue
                    dve.wait_ge(hstep_done, 4 * g + c)
                    nc.vector.tensor_tensor(by_head(hprev[:, c, :]), by_head(hprev[:, c - 1, :]),
                                            cdec[:, 4 * g:4 * g + 4, c].unsqueeze(2).broadcast_to([P, 4, HD]), ALU.mult)\
                      .then_inc(hchain, 1)
                    dve.wait_ge(hchain, 3 * g + c)
                    nc.vector.tensor_tensor(hprev[:, c, :], hprev[:, c, :], bank, ALU.add).then_inc(hstep_done, 1)

            def combine(g):
                for i in range(2):
                    n = 3 * (2 * g + i)
                    dve.wait_ge(yoff_done, 2 * g + i + 1)
                    dve.wait_ge(ef_done, 2 * g + i + 1)
                    nc.vector.tensor_tensor(abc[:, 0, i, CH:TP], ps[:, 5 + i, CH:TP], abc[:, 0, i, CH:TP], ALU.mult)\
                      .then_inc(cchain, 1)
                    if i == 0:
                        dve.wait_ge(sred_done, 4 * g + 4)
                    nc.vector.scalar_tensor_tensor(out=work[:, i, TP:T], in0=act[:, g % 2, 2 + i, S0:CONV_N:TAPS],
                                                   scalar=dtf[:, 2 * g + i, 16:17], in1=ysmp[:, i, :],
                                                   op0=ALU.mult, op1=ALU.add).then_inc(cchain, 1)
                    dve.wait_ge(cchain, n + 1)
                    dve.wait_ge(y1_done, 2 * g + i + 1)
                    nc.vector.tensor_tensor(work[:, i, CH:TP], work[:, i, CH:TP], abc[:, 0, i, CH:TP], ALU.add)\
                      .then_inc(cchain, 1)
                    dve.wait_ge(cchain, n + 3)
                    dve.wait_ge(z_silu_done, 2 * g + i + 1)
                    nc.vector.tensor_tensor(work[:, i, :], work[:, i, :], zs[:, i, :], ALU.mult)\
                      .then_inc(comb_done, 1)

            def window(g):
                nxt = g + 1
                more = nxt < GROUPS
                split_w(Pair(group_pair(g, 2) + 1))
                evac_unit(g, 4)
                dve.wait_ge(cb_done, g + 1)
                if due(4 * g):
                    dve.wait_ge(m_done, 4 * g)
                nc.vector.tensor_tensor(cbm[:, :, :], ps[:, 4, :].rearrange("p (c q) -> p c q", c=NC),
                                        causal[:, :].unsqueeze(1).broadcast_to([P, NC, CH]), ALU.mult)\
                  .then_inc(cbm_done, 1)
                if due(4 * g):
                    dve.wait_ge(state_added, 8 * g)
                dve.wait_ge(silu_done, 4 * g + 4)
                dve.wait_ge(dtf_landed, 32)
                nc.vector.tensor_tensor(xdts[:, :, :], act[:, g % 2, 2:4, S0:CONV_N:TAPS],
                                        dtf[:, 2 * g:2 * g + 2, 0:NS], ALU.mult).then_inc(xdts_done, 1)
                evac_unit(g, 5)
                for i in range(2):
                    dve.wait_ge(xtr_done, 2 * g + i + 1)
                    if due(4 * g):
                        dve.wait_ge(st_done, 4 * g)
                    nc.vector.tensor_tensor(
                        xdt[:, :, i * P:(i + 1) * P].rearrange("p c (h d) -> p c h d", d=HD),
                        ps[:, 4 + i, :].rearrange("p (c h d) -> p c h d", c=NC, d=HD),
                        tokS[:, 0, :, 4 * g + 2 * i:4 * g + 2 * i + 2].unsqueeze(3).broadcast_to([P, NC, 2, HD]),
                        ALU.mult).then_inc(xdt_done, 1)
                decayed(g, 0)
                y_norm(g - 1)
                split_w(Pair(group_pair(nxt, 1) if more else J_OUT1 + 1))
                if not more:
                    y_low(g - 1)
                    sample(g, 0)
                evac_unit(nxt, 0)
                decayed(g, 1)
                y_diag(g, 0)
                if more:
                    conv(nxt, 0)
                evac_unit(nxt, 1)
                sample(g, 0 if more else 1)
                split_w(Pair(group_pair(nxt, 1) + 1 if more else J_OUT1 + 2))
                if more:
                    conv(nxt, 1)
                dve.wait_ge(ydiag_done, 2 * g + 2)
                nc.vector.tensor_tensor(xdt[:, :, :].rearrange("p c (h d) -> p c h d", d=HD),
                                        xdt[:, :, :].rearrange("p c (h d) -> p c h d", d=HD),
                                        tokS[:, 1, :, 4 * g:4 * g + 4].unsqueeze(3).broadcast_to([P, NC, 4, HD]),
                                        ALU.mult).then_inc(xdte_done, 1)
                y_diag(g, 1)
                evac_unit(nxt, 2)
                if more:
                    sample(g, 1)
                if more:
                    conv(nxt, 2)
                if g == 0:
                    dve.wait_ge(cdec_landed, 16)
                states(g)
                sample(g, 2)
                evac_unit(nxt, 3)
                if more:
                    conv(nxt, 3)
                sample(g, 3)
                combine(g)

            evac_scaled(Pair(J_DT), 1, dt_v[:, :], HEADS)
            dve.wait_ge(evac_done, 1)
            dve.wait_ge(par_landed, 48)
            dve.wait_ge(const_ready, 4)
            nc.vector.tensor_scalar(dt_v[:, :], dt_v[:, :], dt_par[:, 0:1], None, ALU.add).then_inc(dt_vec_done, 1)
            nc.vector.tensor_copy(dt_small[:, 16:17], dt_par[:, 2:3]).then_inc(dt_vec_done, 1)
            split_w(Pair(2))
            evac_unit(0, 0)
            evac_unit(0, 1)
            dve.wait_ge(dt_act_done, 4)
            dve.wait_ge(dt_vec_done, 2)
            nc.vector.scalar_tensor_tensor(out=dt_dt[:, :], in0=dt_v[:, :], scalar=0.0, in1=dt_e[:, :],
                                           op0=ALU.max, op1=ALU.add).then_inc(dt_vec_done, 1)
            dve.wait_ge(dt_vec_done, 3)
            nc.vector.tensor_scalar(dt_v[:, :], dt_dt[:, :], dt_par[:, 1:2], -1.0, ALU.mult, ALU.mult).then_inc(dt_vec_done, 1)
            dve.wait_ge(dt_vec_done, 4)
            for c in range(NC):
                cc = slice(c * CH, (c + 1) * CH)
                nc.vector.tensor_tensor_scan(dt_a[:, cc], dt_one[:, :], dt_v[:, cc], 0.0, ALU.mult, ALU.add)\
                  .then_inc(dt_vec_done, 1)
            nc.vector.tensor_copy(dt_small[:, 0:NS], dt_dt[:, TP:T]).then_inc(dt_vec_done, 1)
            conv(0, 0)
            dve.wait_ge(dt_tr_done, 1)
            nc.vector.tensor_copy(tokS[:, :, :, :].rearrange("p a c h -> p (a c h)"), ps[:, 4, 0:3 * NC * HEADS])\
              .then_inc(dt_tok_done, 1)
            dve.wait_ge(dt_tok_done, 1)
            conv(0, 1)
            evac_unit(0, 2)
            split_w(Pair(3))
            evac_unit(0, 3)
            conv(0, 2)
            conv(0, 3)
            for g in range(5):
                window(g)

            def out_product(J, n=None, gain=None):
                for i in range(4):
                    split_w(Pair(J + i + 1))
                    for half in range(2):
                        m = 2 * i + half
                        evac_added(Pair(J + i), half, m)
                        if n is not None and m:
                            h_low(n, m - 1, gain)
                if n is not None:
                    h_low(n, KT - 1, gain)

            out_product(J_OUT0)
            for g in range(5, GROUPS):
                window(g)
            split_w(Pair(J_OUT1 + 3))
            evac_unit(GROUPS, 4)
            evac_unit(GROUPS, 5)
            split_w(Pair(J_TAIL))
            y_norm(7)
            evac_unit(GROUPS, 6)
            y_low(7)
            evac_unit(GROUPS, 7)
            split_w(Pair(J_MLP0))
            for m in range(KT):
                dve.wait_ge(unit_done, Pair(J_TAIL).unit(0, m + 1))
                nc.vector.tensor_tensor(halves(xT[:, m, :]), psum_tok(1 - m % 2), halves(xT[:, m, :]), ALU.add)\
                  .then_inc(evac_done, 1)
                if m:
                    h_low(1, m - 1, G_MLP)
            h_low(1, KT - 1, G_MLP)

            def a_low(j, count, src):
                dve.wait_ge(a_hi_done, count)
                nc.vector.tensor_tensor(a_lo[:, j % 8, :], src, a_hi[:, j % 8, :].bitcast(F32), ALU.subtract)\
                  .then_inc(a_lo_done, 1)

            def mlp(n, J, last):
                base = 0 if n == 1 else 48

                def chunk(c, first, final):
                    for i in range(4):
                        split_w(Pair(J + i + 1, c * 4))
                        if first and i == 0:
                            inv_rms(n)
                        for half in range(2):
                            j = 2 * i + half
                            U = Pair(J + i, c * 4)
                            t = work[:, half, :]
                            if due(c * 8 + (base + j - 1)):
                                dve.wait_ge(a_lo_done, c * 8 + (base + j - 1))
                                dve.wait_ge(a_hi_done, c * 8 + (base + j - 1))
                            evac_scaled(U, half, t)
                            if j:
                                a_low(j - 1, c * 8 + (base + j), work[:, 1 - half, :])
                            dve.wait_ge(evac_done, U.unit(half, 1))
                            nc.vector.scalar_tensor_tensor(out=t, in0=t, scalar=0.0, in1=t, op0=ALU.max, op1=ALU.mult)\
                              .then_inc(a32_done, 1)
                    a_low(7, c * 8 + (base + 8), work[:, 1, :])
                    for i in range(4):
                        if not (final and last and i == 3):
                            split_w(Pair(J + 4 + i + 1, c * 4))
                        for half in range(2):
                            m = 2 * i + half
                            U = Pair(J + 4 + i, c * 4)
                            evac_added(U, half, m)
                            if final and not last and m:
                                h_low(n + 1, m - 1, G_MIX + KT)
                            if final and last:
                                dve.wait_ge(evac_done, U.unit(half, 1))
                                if due(2 * (m - 1)):
                                    dve.wait_ge(ty_done, 2 * (m - 1))
                                nc.vector.tensor_scalar(xg[:, m % 2, :], xT[:, m, :], feat[:, G_FIN + m:G_FIN + m + 1],
                                                        None, ALU.mult).then_inc(xg_done, 1)
                                if m > 1:
                                    y_rows(m - 2)
                    if final and not last:
                        h_low(n + 1, KT - 1, G_MIX + KT)

                chunk(0, True, False)
                with dve.Fori(1, CHUNKS - 1) as c:
                    chunk(c, False, False)
                chunk(CHUNKS - 1, False, True)

            def y_rows(m):
                dve.wait_ge(ty_done, 2 * m + 2)
                nc.vector.tensor_copy(ytok[:, :, m * P:(m + 1) * P], ps[:, 4 + m % 2, :].rearrange("p (c f) -> p c f", c=NC))\
                  .then_inc(ty_evac, 1)

            mlp(1, J_MLP0, False)

            for i in range(8):
                split_w(Pair(J_V + i + 1))
                if i == 0:
                    inv_rms(2)
                for half in range(2):
                    j = 2 * i + half
                    if due(j - 1):
                        dve.wait_ge(gelu_done, j - 1)
                    evac_scaled(Pair(J_V + i), half, work[:, j % 2, :])
                    if j == 2:
                        dve.wait_ge(mixT_done, 1)
                        for n in range(2):
                            nc.vector.tensor_tensor(wmixT[:, 4 * n:4 * n + 4, :],
                                                    ps[:, 6 + n, :].rearrange("p (g t) -> p g t", t=P),
                                                    causal[:, :].unsqueeze(1).broadcast_to([P, 4, CH]), ALU.mult)\
                              .then_inc(wmask_done, 1)
                    if j:
                        dve.wait_ge(v_tr, j)
                        nc.vector.tensor_copy(vtok[:, :, (j - 1) * P:j * P],
                                              ps[:, 4 + (j - 1) % 2, :].rearrange("p (c f) -> p c f", c=NC))\
                          .then_inc(vtok_done, 1)
            dve.wait_ge(v_tr, 16)
            nc.vector.tensor_copy(vtok[:, :, 15 * P:16 * P], ps[:, 5, :].rearrange("p (c f) -> p c f", c=NC))\
              .then_inc(vtok_done, 1)

            def v_scale():
                dve.wait_ge(vroot_done, 2)
                nc.vector.reciprocal(r_tok[:, :], r_tok[:, :]).then_inc(vrec_done, 1)
                nc.vector.reciprocal(r_smp[:, :], r_smp[:, :]).then_inc(vrec_done, 1)
                dve.wait_ge(vrec_done, 2)
                dve.wait_ge(vtok_done, 16)
                for c in range(2):
                    nc.vector.tensor_scalar(vtok[:, c, :], vtok[:, c, :], r_tok[:, c:c + 1], None, ALU.mult)\
                      .then_inc(vscaled, 1)

            def v_samples():
                dve.wait_ge(vsmp_done, 16)
                dve.wait_ge(b_landed, 32)
                nc.vector.tensor_tensor(vsmp[:, :, :], vsmp[:, :, :], r_smp[:, :].unsqueeze(1).broadcast_to([P, 16, NS]),
                                        ALU.mult).then_inc(vsn_done, 1)
                dve.wait_ge(vsn_done, 1)
                nc.vector.tensor_tensor(vsmp[:, :, :], vsmp[:, :, :],
                                        feat[:, G_V:G_V + 16].unsqueeze(2).broadcast_to([P, 16, NS]), ALU.mult)\
                  .then_inc(vsn_done, 1)
                dve.wait_ge(vsn_done, 2)
                by_group = "p (g i) b -> p g (i b)"
                nc.vector.tensor_tensor(ssmp.rearrange(by_group, i=2), vsmp.rearrange(by_group, i=2),
                                        w00[:, :, 0].unsqueeze(2).broadcast_to([P, 8, 2 * NS]), ALU.mult)\
                  .then_inc(ssmp_done, 1)
                dve.wait_ge(ssmp_done, 1)
                nc.vector.tensor_tensor(ssmp.rearrange(by_group, i=2), ssmp.rearrange(by_group, i=2),
                                        bmix[:, :, 0].unsqueeze(2).broadcast_to([P, 8, 2 * NS]), ALU.add)\
                  .then_inc(ssmp_done, 1)
                dve.wait_ge(ssmp_done, 2)

            def u_half(first, J):
                for i in range(4):
                    split_w(Pair(J + i + 1))
                    for half in range(2):
                        j = first + 2 * i + half
                        u, s = work[:, j % 2, :], sq[:, j % 2, :]
                        dve.wait_ge(a32_done, 32 + j - 1)
                        evac_scaled(Pair(J + i), half, u)
                        if j == 0:
                            v_scale()
                            v_samples()
                        if j > first:
                            a_low(j - 1, 32 + j, sq[:, 1 - j % 2, :])
                        dve.wait_ge(mixed, j + 1)
                        dve.wait_ge(a_hi_done, 32 + j - 1)
                        dve.wait_ge(a_lo_done, 32 + j - 1)
                        dve.wait_ge(vsum_done, 15)
                        nc.vector.scalar_tensor_tensor(
                            out=s[:, 0:TP].rearrange("p (c t) -> p c t", c=NC),
                            in0=ps[:, 4 + j % 2, :].rearrange("p (c t) -> p c t", c=NC),
                            scalar=feat[:, G_V + j:G_V + j + 1],
                            in1=bmix[:, j // 2, :].unsqueeze(1).broadcast_to([P, NC, CH]),
                            op0=ALU.mult, op1=ALU.add).then_inc(s_done, 1)
                        dve.wait_ge(s_done, j + 1)
                        dve.wait_ge(gelu_done, 16 + j + 1)
                        nc.vector.tensor_tensor(s[:, TP:T], ssmp[:, j, :], u[:, TP:T], ALU.mult).then_inc(gate_done, 1)
                        nc.vector.tensor_tensor(s[:, 0:TP], s[:, 0:TP], u[:, 0:TP], ALU.mult).then_inc(a32_done, 1)
                        if j in (2, 3, 4, 5):
                            n = j - 2
                            dve.wait_ge(vs_tr, n + 1)
                            if due(16 * n):
                                dve.wait_ge(vs_out, 16 * n)
                            nc.vector.tensor_copy(vs_row[:, :, :].rearrange("p a b -> p (a b)"), ps[0:NS, 6 + n % 2, :])\
                              .then_inc(vs_evac, 1)
                dve.wait_ge(a32_done, 32 + first + 8)
                dve.wait_ge(gate_done, first + 8)
                a_low(first + 7, 32 + first + 8, sq[:, 1, :])

            u_half(0, J_U0)
            out_product(J_CMO0)
            u_half(8, J_U1)
            out_product(J_CMO1, 3, G_MLP + KT)
            dve.wait_ge(vs_out, 64)
            mlp(3, J_MLP1, True)
            y_rows(6)
            y_rows(7)
            nc.vector.tensor_copy(ys_row[:, :].rearrange("p (a f) -> p a f", a=2), ps[0:NS, 6:8, :]).then_inc(ty_evac, 1)
            dve.wait_ge(fin_root, 2)
            nc.vector.reciprocal(r_fin[:, 0:NC], r_fin[:, 0:NC]).then_inc(fin_rec, 1)
            nc.vector.reciprocal(r_fin[0:NS, NC:NC + 1], r_fin[0:NS, NC:NC + 1]).then_inc(fin_rec, 1)
            dve.wait_ge(fin_rec, 2)
            dve.wait_ge(ty_evac, 9)
            for c in range(0, NC, 2):
                nc.vector.tensor_scalar(ytok[:, c, :], ytok[:, c, :], r_fin[:, c:c + 1], None, ALU.mult)\
                  .then_inc(y_scaled, 1)
            nc.vector.tensor_scalar(ys_row[:, :], ys_row[:, :], r_fin[0:NS, NC:NC + 1], None, ALU.mult)\
              .then_inc(y_scaled, 1)


_INS = ("x_prompt x_sample state_ssm state_conv norm_mix_g norm_mlp_g norm_final_g ssd_w_in ssd_conv_w "
        "ssd_conv_b ssd_dt_bias ssd_a_log ssd_d ssd_norm_g ssd_w_out cm_w_in cm_b_in cm_v_norm_g cm_w_s "
        "cm_b_s cm_w_out mlp_w_up mlp_w_down").split()
_OUTS = ((1, TP, D), (NS, 1, D), (1, 1, HEADS, HD, N), (1, 1, TAPS - 1, CONVD), (1, NS, HEADS, HD, N),
         (1, NS, TAPS - 1, CONVD), (1, NS, 1, CMW))


def kernel(**inputs):
    import numpy as np
    import concourse.bacc as bacc
    from concourse.bass_utils import run_bass_kernel_spmd

    nc = bacc.Bacc("TRN2", target_bir_lowering=False, num_devices=1)
    arrays, args = {}, []
    for name in _INS:
        a = np.ascontiguousarray(inputs[name])
        arrays["in_" + name] = a
        args.append(nc.dram_tensor("in_" + name, a.shape, mybir.dt.from_np(a.dtype), kind="ExternalInput").ap())
    for i, shape in enumerate(_OUTS):
        args.append(nc.dram_tensor(f"out_{i}", shape, F32, kind="ExternalOutput").ap())
    hybrid_step(nc, *args)
    r = run_bass_kernel_spmd(nc, [arrays], core_ids=[0])
    return tuple(r.results[0][f"out_{i}"] for i in range(len(_OUTS)))
```
